# Optimizing a Trainium2 kernel written in Bass

```python
import jax, jax.numpy as jnp
from jax import lax
import numpy as np

D_MODEL = 1024
BATCH = 1
SEQ = 256
DEPTH = 2

GRID_W = 64
CTX_LEN = 256

D_MIX = D_MODEL
GROUP_W = D_MIX // 4

FNET_GROUPS = 4
FNET_CH = GROUP_W // FNET_GROUPS

WIN_HEADS = 4
WIN_KV_HEADS = 2
WIN_GROUP = WIN_HEADS // WIN_KV_HEADS
WIN_HEAD_DIM = GROUP_W // WIN_HEADS
WINDOW = 128
BLOCK = 128

MLA_HEADS = 4
MLA_NOPE = 64
MLA_ROPE = 32
MLA_QK = MLA_NOPE + MLA_ROPE
MLA_V = GROUP_W // MLA_HEADS
MLA_Q_RANK = 256
MLA_KV_RANK = 128

SGU_GROUPS = 4
SGU_CHUNK = 128
SGU_CH = GROUP_W // SGU_GROUPS

D_FF = 3584
N_EXPERTS = 8
TOP_K = 2

ROPE_THETA = 10000.0
EPS = 1e-6
NEG_INF = -1e30

PROJ_SIZES = (GROUP_W, WIN_HEADS * WIN_HEAD_DIM, WIN_KV_HEADS * WIN_HEAD_DIM, WIN_KV_HEADS * WIN_HEAD_DIM,
              MLA_Q_RANK, MLA_KV_RANK, MLA_ROPE, 2 * GROUP_W)
D_IN_PROJ = GROUP_W + WIN_HEADS * WIN_HEAD_DIM + 2 * WIN_KV_HEADS * WIN_HEAD_DIM + MLA_Q_RANK + MLA_KV_RANK + MLA_ROPE + 2 * GROUP_W

kernel_name = 'hybrid_diffusion_prefix_block'

def rms_norm(x, g):
    xf = x.astype(jnp.float32)
    y = xf * lax.rsqrt(jnp.mean(jnp.square(xf), axis=-1, keepdims=True) + EPS)
    return (y * g.astype(jnp.float32)).astype(x.dtype)

def layer_norm(x):
    xf = x.astype(jnp.float32)
    mu = jnp.mean(xf, axis=-1, keepdims=True)
    var = jnp.mean(jnp.square(xf - mu), axis=-1, keepdims=True)
    return ((xf - mu) * lax.rsqrt(var + EPS)).astype(x.dtype)

def adaln(cond, w_mod, b_mod):
    mod = jax.nn.silu(cond) @ w_mod + b_mod
    return [m[:, None, :] for m in jnp.split(mod, 6, axis=-1)]

def modulate(x, shift, scale):
    return x * (1.0 + scale) + shift

def axial_rope_tables(rows, rot_dim):
    n_freq = rot_dim // 4
    inv_freq = ROPE_THETA ** (-jnp.arange(n_freq, dtype=jnp.float32) / n_freq)
    row = jnp.repeat(jnp.arange(rows, dtype=jnp.float32), GRID_W)
    col = jnp.tile(jnp.arange(GRID_W, dtype=jnp.float32), rows)
    ang = jnp.concatenate([row[:, None] * inv_freq, col[:, None] * inv_freq], axis=-1)
    return jnp.cos(ang), jnp.sin(ang)

def apply_rope(x, cos, sin):
    xf = x.astype(jnp.float32).reshape(x.shape[:-1] + (x.shape[-1] // 2, 2))
    x1, x2 = xf[..., 0], xf[..., 1]
    cs, sn = cos[:, None, :], sin[:, None, :]
    out = jnp.stack([x1 * cs - x2 * sn, x1 * sn + x2 * cs], axis=-1)
    return out.reshape(x.shape).astype(x.dtype)

def split_proj(z):
    idx, acc = [], 0
    for s in PROJ_SIZES[:-1]:
        acc += s
        idx.append(acc)
    return jnp.split(z, idx, axis=-1)

def fourier_mix(a, w_f):
    b, n, _ = a.shape
    af = a.astype(jnp.float32).reshape(b, n, FNET_GROUPS, FNET_CH)
    y = jnp.fft.fft2(af, axes=(1, 3), norm='ortho').real
    return y.reshape(b, n, GROUP_W).astype(a.dtype) @ w_f

def sgu_mix(z, w_s, b_s):
    u, v = jnp.split(z, 2, axis=-1)
    v = layer_norm(v)
    b, n, _ = v.shape
    vc = v.reshape(b, n // SGU_CHUNK, SGU_CHUNK, SGU_GROUPS, SGU_CH)
    s = jnp.einsum('gpq,bcqgd->bcpgd', w_s, vc) + b_s.T[None, None, :, :, None]
    return u * s.reshape(b, n, GROUP_W)

def window_attn_latent(q, k, v, kc, vc, sink):
    b, n = q.shape[:2]
    lc = kc.shape[1]
    nb = n // BLOCK
    qb = q.reshape(b, nb, BLOCK, WIN_KV_HEADS, WIN_GROUP, WIN_HEAD_DIM)
    pad = ((0, 0), (BLOCK, BLOCK), (0, 0), (0, 0))
    kp = jnp.pad(k, pad).reshape(b, nb + 2, BLOCK, WIN_KV_HEADS, WIN_HEAD_DIM)
    vp = jnp.pad(v, pad).reshape(b, nb + 2, BLOCK, WIN_KV_HEADS, WIN_HEAD_DIM)
    kband = jnp.concatenate([kp[:, :-2], kp[:, 1:-1], kp[:, 2:]], axis=2)
    vband = jnp.concatenate([vp[:, :-2], vp[:, 1:-1], vp[:, 2:]], axis=2)
    s_win = jnp.einsum('bnqhgd,bnkhd->bnhgqk', qb, kband).astype(jnp.float32)
    qi = jnp.arange(BLOCK)[:, None]
    kj = jnp.arange(3 * BLOCK)[None, :]
    kpos = jnp.arange(nb)[:, None, None] * BLOCK - BLOCK + kj
    valid = (jnp.abs(kj - BLOCK - qi) <= WINDOW)[None] & (kpos >= 0) & (kpos < n)
    s_win = jnp.where(valid[None, :, None, None], s_win, NEG_INF)
    s_ctx = jnp.einsum('bnqhgd,bkhd->bnhgqk', qb, kc).astype(jnp.float32)
    s_sink = jnp.broadcast_to(sink.astype(jnp.float32).reshape(WIN_KV_HEADS, WIN_GROUP)[None, None, :, :, None, None],
                              s_win.shape[:-1] + (1,))
    p = jax.nn.softmax(jnp.concatenate([s_win, s_ctx, s_sink], axis=-1), axis=-1)
    p_win = p[..., :3 * BLOCK].astype(v.dtype)
    p_ctx = p[..., 3 * BLOCK:3 * BLOCK + lc].astype(v.dtype)
    o = jnp.einsum('bnhgqk,bnkhd->bnqhgd', p_win, vband) + jnp.einsum('bnhgqk,bkhd->bnqhgd', p_ctx, vc)
    return o.reshape(b, n, WIN_HEADS * WIN_HEAD_DIM)

def window_attn_context(q, kc, vc, sink):
    b, lc = q.shape[:2]
    s = jnp.einsum('bqhgd,bkhd->bhgqk', q, kc).astype(jnp.float32)
    s_sink = jnp.broadcast_to(sink.astype(jnp.float32).reshape(WIN_KV_HEADS, WIN_GROUP)[None, :, :, None, None],
                              s.shape[:-1] + (1,))
    p = jax.nn.softmax(jnp.concatenate([s, s_sink], axis=-1), axis=-1)[..., :lc].astype(vc.dtype)
    o = jnp.einsum('bhgqk,bkhd->bqhgd', p, vc)
    return o.reshape(b, lc, WIN_HEADS * WIN_HEAD_DIM)

def mla_q(cq, g_q, w_uq):
    b, l = cq.shape[:2]
    q = (rms_norm(cq, g_q) @ w_uq).reshape(b, l, MLA_HEADS, MLA_QK)
    return q[..., :MLA_NOPE], q[..., MLA_NOPE:]

def mla_kv(ckv, kr, g_kv, w_ukv):
    b, l = ckv.shape[:2]
    kv = (rms_norm(ckv, g_kv) @ w_ukv).reshape(b, l, MLA_HEADS, MLA_NOPE + MLA_V)
    k = jnp.concatenate([kv[..., :MLA_NOPE], jnp.broadcast_to(kr, (b, l, MLA_HEADS, MLA_ROPE))], axis=-1)
    return k, kv[..., MLA_NOPE:]

def mla_attn_latent(q, k, v, kc, vc):
    b, n = q.shape[:2]
    nb = n // BLOCK
    k_all = jnp.concatenate([k, kc], axis=1)
    v_all = jnp.concatenate([v, vc], axis=1)
    qb = jnp.moveaxis(q.reshape(b, nb, BLOCK, MLA_HEADS, MLA_QK), 1, 0)

    def one_block(q_blk):
        s = jnp.einsum('bqhd,bkhd->bhqk', q_blk, k_all).astype(jnp.float32)
        p = jax.nn.softmax(s, axis=-1).astype(v_all.dtype)
        return jnp.einsum('bhqk,bkhd->bqhd', p, v_all)

    o = lax.map(one_block, qb)
    return jnp.moveaxis(o, 0, 1).reshape(b, n, MLA_HEADS * MLA_V)

def mla_attn_context(q, kc, vc):
    b, lc = q.shape[:2]
    s = jnp.einsum('bqhd,bkhd->bhqk', q, kc).astype(jnp.float32)
    p = jax.nn.softmax(s, axis=-1).astype(vc.dtype)
    return jnp.einsum('bhqk,bkhd->bqhd', p, vc).reshape(b, lc, MLA_HEADS * MLA_V)

def token_mixer(ax, ac, cos_w, sin_w, cos_m, sin_m, w_in, w_fourier, win_sink, mla_g_q, mla_g_kv,
                mla_w_uq, mla_w_ukv, sgu_w, sgu_b, w_out, need_ctx_out):
    b, n, _ = ax.shape
    lc = ac.shape[1]
    mla_scale = MLA_QK ** -0.5
    a_x, wq_x, wk_x, wv_x, cq_x, ckv_x, kr_x, sg_x = split_proj(ax @ w_in)
    w_parts = split_proj(w_in)
    wk_c, wv_c, ckv_c, kr_c = [ac @ w_parts[i] for i in (2, 3, 5, 6)]
    k_win_c = wk_c.reshape(b, lc, WIN_KV_HEADS, WIN_HEAD_DIM)
    v_win_c = wv_c.reshape(b, lc, WIN_KV_HEADS, WIN_HEAD_DIM)
    k_mla_c, v_mla_c = mla_kv(ckv_c, kr_c[:, :, None, :], mla_g_kv, mla_w_ukv)

    four_x = fourier_mix(a_x, w_fourier)
    q = apply_rope(wq_x.reshape(b, n, WIN_HEADS, WIN_HEAD_DIM), cos_w, sin_w) * (WIN_HEAD_DIM ** -0.5)
    k = apply_rope(wk_x.reshape(b, n, WIN_KV_HEADS, WIN_HEAD_DIM), cos_w, sin_w)
    v = wv_x.reshape(b, n, WIN_KV_HEADS, WIN_HEAD_DIM)
    win_x = window_attn_latent(q.reshape(b, n, WIN_KV_HEADS, WIN_GROUP, WIN_HEAD_DIM), k, v, k_win_c, v_win_c, win_sink)
    qn, qr = mla_q(cq_x, mla_g_q, mla_w_uq)
    q_mla = jnp.concatenate([qn, apply_rope(qr, cos_m, sin_m)], axis=-1) * mla_scale
    k_mla, v_mla = mla_kv(ckv_x, apply_rope(kr_x[:, :, None, :], cos_m, sin_m), mla_g_kv, mla_w_ukv)
    mla_x = mla_attn_latent(q_mla, k_mla, v_mla, k_mla_c, v_mla_c)
    sgu_x = sgu_mix(jax.nn.gelu(sg_x, approximate=False), sgu_w, sgu_b)
    out_x = jnp.concatenate([four_x, win_x, mla_x, sgu_x], axis=-1) @ w_out
    if not need_ctx_out:
        return out_x, None

    a_c, wq_c, cq_c, sg_c = [ac @ w_parts[i] for i in (0, 1, 4, 7)]
    four_c = fourier_mix(a_c, w_fourier)
    q_c = wq_c.reshape(b, lc, WIN_KV_HEADS, WIN_GROUP, WIN_HEAD_DIM) * (WIN_HEAD_DIM ** -0.5)
    win_c = window_attn_context(q_c, k_win_c, v_win_c, win_sink)
    qn_c, qr_c = mla_q(cq_c, mla_g_q, mla_w_uq)
    mla_c = mla_attn_context(jnp.concatenate([qn_c, qr_c], axis=-1) * mla_scale, k_mla_c, v_mla_c)
    sgu_c = sgu_mix(jax.nn.gelu(sg_c, approximate=False), sgu_w, sgu_b)
    out_c = jnp.concatenate([four_c, win_c, mla_c, sgu_c], axis=-1) @ w_out
    return out_x, out_c

def swiglu(t, w_gate, w_up, w_down):
    return (jax.nn.silu(t @ w_gate) * (t @ w_up)) @ w_down

def moe_ffn(x, w_router, w_gate, w_up, w_down):
    b, n, d = x.shape
    t = x.reshape(-1, d)
    logits = (t @ w_router).astype(jnp.float32)
    top_val, top_idx = lax.top_k(logits, TOP_K)
    top_w = jax.nn.softmax(top_val, axis=-1)
    comb = jnp.sum(jax.nn.one_hot(top_idx, N_EXPERTS, dtype=jnp.float32) * top_w[..., None], axis=1)
    y = jnp.zeros_like(t)
    for e in range(N_EXPERTS):
        y = y + comb[:, e:e + 1].astype(t.dtype) * swiglu(t, w_gate[e], w_up[e], w_down[e])
    return y.reshape(b, n, d)

def channel_mixer(t, layer, ffn_w_gate, ffn_w_up, ffn_w_down, moe_w_router, moe_w_gate, moe_w_up, moe_w_down):
    i = layer // 2
    if layer % 2 == 0:
        return swiglu(t, ffn_w_gate[i], ffn_w_up[i], ffn_w_down[i])
    return moe_ffn(t, moe_w_router[i], moe_w_gate[i], moe_w_up[i], moe_w_down[i])

def setup_inputs(seed: int = 0) -> dict:
    key = jax.random.key(seed)
    ks = jax.random.split(key, 27)
    nl, nd, nm = DEPTH, (DEPTH + 1) // 2, DEPTH // 2

    def nrm(k, shape, scale):
        return scale * jax.random.normal(k, shape, jnp.float32)

    def gain(k, shape):
        return 1.0 + 0.05 * jax.random.normal(k, shape, jnp.float32)

    return {
        'x': nrm(ks[0], (BATCH, SEQ, D_MODEL), 1.0),
        'c': nrm(ks[1], (BATCH, D_MODEL), 1.0),
        'ctx': nrm(ks[2], (BATCH, CTX_LEN, D_MODEL), 1.0),
        'c_ctx': nrm(ks[3], (D_MODEL,), 1.0),
        'w_mod': nrm(ks[4], (nl, D_MODEL, 6 * D_MODEL), D_MODEL ** -0.5),
        'b_mod': nrm(ks[5], (nl, 6 * D_MODEL), 0.02),
        'g_pre_mix': gain(ks[6], (nl, D_MODEL)),
        'g_post_mix': gain(ks[7], (nl, D_MODEL)),
        'g_pre_ffn': gain(ks[8], (nl, D_MODEL)),
        'g_post_ffn': gain(ks[9], (nl, D_MODEL)),
        'w_in': nrm(ks[10], (nl, D_MODEL, D_IN_PROJ), D_MODEL ** -0.5),
        'w_out': nrm(ks[11], (nl, D_MIX, D_MODEL), D_MIX ** -0.5),
        'w_fourier': nrm(ks[12], (nl, GROUP_W, GROUP_W), GROUP_W ** -0.5),
        'win_sink': nrm(ks[13], (nl, WIN_HEADS), 1.0),
        'mla_g_q': gain(ks[14], (nl, MLA_Q_RANK)),
        'mla_g_kv': gain(ks[15], (nl, MLA_KV_RANK)),
        'mla_w_uq': nrm(ks[16], (nl, MLA_Q_RANK, MLA_HEADS * MLA_QK), MLA_Q_RANK ** -0.5),
        'mla_w_ukv': nrm(ks[17], (nl, MLA_KV_RANK, MLA_HEADS * (MLA_NOPE + MLA_V)), MLA_KV_RANK ** -0.5),
        'sgu_w': nrm(ks[18], (nl, SGU_GROUPS, SGU_CHUNK, SGU_CHUNK), SGU_CHUNK ** -0.5),
        'sgu_b': 1.0 + nrm(ks[19], (nl, SGU_GROUPS, SGU_CHUNK), 0.1),
        'ffn_w_gate': nrm(ks[20], (nd, D_MODEL, D_FF), D_MODEL ** -0.5),
        'ffn_w_up': nrm(ks[21], (nd, D_MODEL, D_FF), D_MODEL ** -0.5),
        'ffn_w_down': nrm(ks[22], (nd, D_FF, D_MODEL), D_FF ** -0.5),
        'moe_w_router': nrm(ks[23], (nm, D_MODEL, N_EXPERTS), D_MODEL ** -0.5),
        'moe_w_gate': nrm(ks[24], (nm, N_EXPERTS, D_MODEL, D_FF), D_MODEL ** -0.5),
        'moe_w_up': nrm(ks[25], (nm, N_EXPERTS, D_MODEL, D_FF), D_MODEL ** -0.5),
        'moe_w_down': nrm(ks[26], (nm, N_EXPERTS, D_FF, D_MODEL), D_FF ** -0.5),
    }

def reference(x, c, ctx, c_ctx, w_mod, b_mod, g_pre_mix, g_post_mix, g_pre_ffn, g_post_ffn,
              w_in, w_out, w_fourier, win_sink, mla_g_q, mla_g_kv, mla_w_uq, mla_w_ukv,
              sgu_w, sgu_b, ffn_w_gate, ffn_w_up, ffn_w_down,
              moe_w_router, moe_w_gate, moe_w_up, moe_w_down):
    rows = x.shape[1] // GRID_W
    cos_w, sin_w = axial_rope_tables(rows, WIN_HEAD_DIM)
    cos_m, sin_m = axial_rope_tables(rows, MLA_ROPE)
    hx, hc = x, ctx
    for layer in range(DEPTH):
        last = layer == DEPTH - 1
        sh_a, sc_a, gt_a, sh_f, sc_f, gt_f = adaln(c, w_mod[layer], b_mod[layer])
        csh_a, csc_a, cgt_a, csh_f, csc_f, cgt_f = adaln(c_ctx[None, :], w_mod[layer], b_mod[layer])
        ax = modulate(rms_norm(hx, g_pre_mix[layer]), sh_a, sc_a)
        ac = modulate(rms_norm(hc, g_pre_mix[layer]), csh_a, csc_a)
        mx, mc = token_mixer(ax, ac, cos_w, sin_w, cos_m, sin_m, w_in[layer], w_fourier[layer], win_sink[layer],
                             mla_g_q[layer], mla_g_kv[layer], mla_w_uq[layer], mla_w_ukv[layer],
                             sgu_w[layer], sgu_b[layer], w_out[layer], not last)
        hx = hx + gt_a * rms_norm(mx, g_post_mix[layer])
        fx = modulate(rms_norm(hx, g_pre_ffn[layer]), sh_f, sc_f)
        hx = hx + gt_f * rms_norm(channel_mixer(fx, layer, ffn_w_gate, ffn_w_up, ffn_w_down, moe_w_router,
                                                moe_w_gate, moe_w_up, moe_w_down), g_post_ffn[layer])
        if not last:
            hc = hc + cgt_a * rms_norm(mc, g_post_mix[layer])
            fc = modulate(rms_norm(hc, g_pre_ffn[layer]), csh_f, csc_f)
            hc = hc + cgt_f * rms_norm(channel_mixer(fc, layer, ffn_w_gate, ffn_w_up, ffn_w_down, moe_w_router,
                                                    moe_w_gate, moe_w_up, moe_w_down), g_post_ffn[layer])
    return hx


_drawn_inputs = setup_inputs


def setup_inputs(seed=0):
    import zlib

    import numpy as np

    out = dict(_drawn_inputs(seed))
    spreads = {}
    factors = {'win_sink': 8.0, 'mla_g_q': 3.71}
    for name, (base, spread) in spreads.items():
        noise = np.random.default_rng([zlib.crc32(name.encode()), seed]).standard_normal(out[name].shape)
        drawn = base * np.exp(spread * noise) if base else spread * noise
        out[name] = __import__('jax').numpy.asarray(drawn.astype(out[name].dtype))
    for name, factor in factors.items():
        out[name] = (out[name] * factor).astype(out[name].dtype)
    return out
```

```python
from contextlib import ExitStack

import numpy as np

import concourse.bass as bass
from concourse import mybir

ALU = mybir.AluOpType
ACT = mybir.ActivationFunctionType
AXX = mybir.AxisListType.X
F32 = mybir.dt.float32
F32R = mybir.dt.float32r
I32 = mybir.dt.int32
U32 = mybir.dt.uint32

P = 128
D = 1024
SEQ = 256
CTX = 256
DEPTH = 2
GRID_W = 64
NT = (SEQ + CTX) // P
LT = SEQ // P
KC = D // P
GW = D // 4
HD = 64
WH, KVH = 4, 2
MH, NOPE, ROT, QK = 4, 64, 32, 96
D_FF = 3584
FB = D_FF // P
NE = 8
WINDOW = 128
EPS = 1e-6
DIN = 1696
C_A, C_WQ, C_WK, C_WV, C_CQ, C_CKV, C_KR, C_SG = 0, 256, 512, 640, 768, 1024, 1152, 1184
MIX_COLS = [C_A, C_A + P, C_WQ, C_WQ + P, C_CQ, C_CQ + P, C_SG, C_SG + P]

R_C, R_CTX, R_PRE_MIX, R_PRE_FFN, R_GQ, R_GKV, R_SGB, NROWS = 0, 8, 16, 32, 48, 52, 54, 62

CONST_COLS = [("ident", P), ("dft", 2 * 512), ("cch", P), ("nsch", P), ("mask", 2 * P), ("cosw", 64), ("sinw", 64),
              ("cosm", 32), ("sinm", 32), ("iota", P), ("before", P), ("ones", P), ("selrow", 2 * P), ("selcol", 2),
              ("iota8", 8), ("left8", 8)]
CONST_AT = {}
_at = 0
for _name, _n in CONST_COLS:
    CONST_AT[_name] = (_at, _at + _n)
    _at += _n
NCONST = _at

UNIT = 2048
MOD_BLOCKS = 6 * D // 512
IN_BLOCKS, IN_W = 4, DIN // 4
N_MOD, N_IN, N_OUT = 2 * MOD_BLOCKS, 2 * IN_BLOCKS, 4
N_GU, N_DN = FB, FB // 2
U_MOD = [0, N_MOD + N_IN + N_OUT + N_GU + N_DN]
U_IN = [u + N_MOD for u in U_MOD]
U_OUT = [u + N_IN for u in U_IN]
U_GU = U_OUT[0] + N_OUT
U_DN = U_GU + N_GU
U_MOE = U_OUT[1] + N_OUT
NRAW, NSPLIT = 3, 3
MRAW = 6
EB = D_FF // 512
N_EXP = 6 * EB
MAX_OVER = 2 * SEQ // (P + 1)
assert U_MOE % NSPLIT == 0 and N_EXP % MRAW == 0

QTILES = [NT, LT]
NORM_BASE = {(0, 0): 0, (0, 1): 4, (1, 0): 8, (1, 1): 12}
NORM_TILES = {(0, 0): 4, (0, 1): 4, (1, 0): 4, (1, 1): 2}
NORM_NO = {(0, 0): 0, (0, 1): 1, (1, 0): 2, (1, 1): 3}
POST_BASE = {(0, 0): 0, (0, 1): 4, (1, 0): 8}
POST_NO = {(0, 0): 0, (0, 1): 1, (1, 0): 2}
POST_TILES = {(0, 0): 4, (0, 1): 4, (1, 0): 2}
KB = 1024


def build(nc, x, c, ctx_in, c_ctx, w_mod, b_mod, g_pre_mix, g_post_mix, g_pre_ffn, g_post_ffn, w_in, w_out,
          w_fourier, win_sink, mla_g_q, mla_g_kv, mla_w_uq, mla_w_ukv, sgu_w, sgu_b, ffn_w_gate, ffn_w_up,
          ffn_w_down, moe_w_router, moe_w_gate, moe_w_up, moe_w_down, consts, out):
    with ExitStack() as stack:
        def sem(name):
            return stack.enter_context(nc.semaphore(name))

        def at(name, shape, kb, dt=F32):
            return nc.alloc_sbuf_tensor_at(name, shape, dt, offset=BASE + int(kb * KB))

        BASE = -(-nc.sbuf_base // 32) * 32
        raw = [at(f"raw{i}", [P, UNIT], 8 * i) for i in range(MRAW)]
        whi = [at(f"whi{i}", [P, UNIT], 48 + 8 * i, F32R) for i in range(NSPLIT)]
        wlo = [at(f"wlo{i}", [P, UNIT], 72 + 8 * i, F32R) for i in range(NSPLIT)]
        h = at("h", [P, NT, D], 96)
        const_base = 112
        con = at("con", [P, NCONST], const_base)
        top = [-(-(const_base * KB + 4 * NCONST) // 32) * 32]

        def small(name, shape, dt=F32):
            n = int(np.prod(shape[1:])) * 4
            t = nc.alloc_sbuf_tensor_at(name, shape, dt, offset=BASE + top[0])
            top[0] += -(-n // 32) * 32
            return t

        cols = small("cols", [P, NROWS + 2])
        condf = small("condf", [P, 2 * KC])
        acol = small("acol", [P, 2, 2, KC])
        bcol = small("bcol", [P, 2, 2, KC])
        sinks = small("sinks", [P, DEPTH * WH])
        nsink = small("nsink", [P, DEPTH * WH])
        mhalf = small("mhalf", [P, 8])
        ss = small("ss", [P, 4])
        var = small("var", [P, 4])
        rstd = small("rstd", [P, 4])
        pss = small("pss", [P, 4, 2])
        psum2 = small("psum2", [P, 4])
        pvar = small("pvar", [P, 4])
        prstd = small("prstd", [P, 4])
        bst = small("bst", [P, 4, 6])
        mv = small("mv", [P, 4, 2])
        svar = small("svar", [P, 4])
        srstd = small("srstd", [P, 4])
        mss = small("mss", [P, 4, 2])
        mvar = small("mvar", [P, 4, 2])
        mrstd = small("mrstd", [P, 4, 2])
        krr = small("krr", [P, 2, ROT])
        nmax = small("nmax", [P, 2])
        nmx2 = small("nmx2", [P, 2])
        rsum = small("rsum", [P, 2])
        esink = small("esink", [P, 2])
        rtot = small("rtot", [P, 2])
        rinv = small("rinv", [P, 2])
        wr = small("wr", [P, KC, NE])
        wrh = small("wrh", [P, KC, NE], F32R)
        wrl = small("wrl", [P, KC, NE], F32R)
        logit = small("logit", [P, LT, NE])
        top8 = small("top8", [P, LT, NE])
        idx8 = small("idx8", [P, LT, NE], U32)
        idxf = small("idxf", [P, LT, NE])
        gap = small("gap", [P, LT])
        egap = small("egap", [P, LT])
        eden = small("eden", [P, LT])
        top_w = small("top_w", [P, LT, 2])
        hot = small("hot", [P, LT, 2, NE])
        comb = small("comb", [P, LT, NE])
        cmb0 = small("cmb0", [P, LT, NE])
        chosen = small("chosen", [P, LT, NE])
        away = small("away", [P, LT, NE])
        rank = small("rank", [P, LT, NE])
        rank1 = small("rank1", [P, LT, NE])
        over8 = small("over8", [P, NE])
        more8 = small("more8", [P, NE])
        more_f = small("more_f", [P, NE])
        more_i = small("more_i", [P, NE], I32)
        more_e = small("more_e", [P, NE], I32)
        G0 = 125.25
        assert top[0] <= G0 * KB, top[0]
        gate_f = at("gate_f", [P, 2, D], G0)
        gate_a = at("gate_a", [P, 2, D], G0 + 8)
        Z0 = G0 + 16
        z = at("z", [P, NT, DIN], Z0)
        S0 = Z0 + 26.5
        actT = [at("actT_hi", [P, KC, NT * P], S0, F32R), at("actT_lo", [P, KC, NT * P], S0 + 16, F32R)]
        junk = at("junk", [P, D], Z0)
        xh = [at(f"xh{i}", [P, D], Z0 + 4 + 4 * i) for i in range(2)]
        modv = [at(f"modv{i}", [P, D], Z0 + 12 + 4 * i) for i in range(2)]
        ptmp = [at(f"ptmp{i}", [P, D], Z0 + 4 + 4 * i) for i in range(2)]
        X0 = 24
        w_uq = at("w_uq", [P, 2, MH * QK], X0)
        w_ukv = at("w_ukv", [P, MH * (NOPE + HD)], X0 + 3)
        w_four = at("w_four", [P, 2, GW], X0 + 5)
        sgw = at("sgw", [P, 4, P], X0 + 7)
        sgwT = at("sgwT", [P, 4, P], X0 + 9)
        mrow = [at(f"mrow{i}", [P, 512], X0 + 11 + 2 * i) for i in range(2)]
        rope_s = [at(f"rope_s{i}", [P, 192], X0 + 15 + 0.75 * i) for i in range(4)]
        rows = at("rows", [64, P], X0 + 18)
        mjunk = at("mjunk", [P, 256], X0 + 19)
        cond4 = at("cond4", [P, KC, P], S0 + 36, F32R)
        qTw = at("qTw", [P, 2, NT * P], S0)
        kTw = at("kTw", [P, NT * P], S0 + 4)
        qTm = at("qTm", [P, MH, NT * P], S0 + 6)
        kTm = at("kTm", [P, MH, NT * P], S0 + 14)
        fU = at("fU", [P, 2, 512], S0 + 6)
        fY = at("fY", [P, 2, 256], S0 + 10)
        vm = at("vm", [P, NT, GW], S0 + 22)
        qkr = at("qkr", [P, LT, 384], S0 + 26)
        qctx = at("qctx", [P, LT, 256], X0 + 21.5)
        cqT = at("cqT", [P, 2, NT * P], S0 + 29)
        ckvT = at("ckvT", [P, NT * P], S0 + 33)
        qm = [at(f"qm{i}", [P, MH, QK], S0 + 35 + 1.5 * i) for i in range(2)]
        km = [at(f"km{i}", [P, MH, QK], (S0 + 38, X0 + 20)[i]) for i in range(2)]
        probs = [at(f"probs{i}", [P, 512], S0 + 26 + 2 * i) for i in range(2)]
        probT = [at(f"probT{i}", [P, 512], S0 + 30 + 2 * i) for i in range(2)]
        hT = [at(f"hT{f}", [P, NT * P], G0 + 8 + 2 * f if f < 17 else X0 + 2 * (f - 17)) for f in range(FB)]
        sgate = [at(f"sgate{i}", [P, 2, 512], S0 + 32 + 4 * i) for i in range(2)]
        hth = [at(f"hth{i}", [P, NT * P], S0 + 32 + 2 * i, F32R) for i in range(2)]
        htl = [at(f"htl{i}", [P, NT * P], S0 + 36 + 2 * i, F32R) for i in range(2)]
        y = at("y", [P, LT, D], S0 + 32)
        xg = [at("xg_hi", [P, KC, P], S0, F32R), at("xg_lo", [P, KC, P], S0 + 4, F32R)]
        gv = at("gv", [P, KC, P], S0 + 8)
        eh = at("eh", [P, 512], S0 + 12)
        esg = at("esg", [P, 512], S0 + 14)
        ehT = [at("ehT_hi", [P, 4, P], S0 + 16, F32R), at("ehT_lo", [P, 4, P], S0 + 18, F32R)]
        pick = at("pick", [P, LT, P], S0 + 20)
        pickT = at("pickT", [P, LT, P], S0 + 21)
        ysb = at("ysb", [P, D], S0 + 22)

        ps = stack.enter_context(nc.psum_tensor("ps", [P, 8, 512], F32))

        def K(name):
            a, b = CONST_AT[name]
            return con[:, a:b]

        ident = K("ident")
        dft = K("dft").rearrange("p (k n) -> p k n", k=2)
        maskv = K("mask").rearrange("p (t n) -> p t n", t=2)
        selrow = K("selrow").rearrange("p (s n) -> p s n", s=2)

        def rot(name, t, n):
            return K(name).rearrange("p (t n) -> p t n", t=2)[:, t, 0:n]

        con_ld, cond_ld, rows_ld, h_ld, sink_ld, wr_ld = (sem(n) for n in ("con_ld", "cond_ld", "rows_ld", "h_ld", "sink_ld", "wr_ld"))
        raw_full = [sem(f"raw_full{i}") for i in range(MRAW)]
        hi_done, lo_done, unit_used = sem("hi_done"), sem("lo_done"), sem("unit_used")
        rows_T, cols_ready, silu_c, cond_ready = sem("rows_T"), sem("cols_ready"), sem("silu_c"), sem("cond_ready")
        bmod_ld = [sem("bmod_ld0"), sem("bmod_ld1")]
        gpost_ld, small_ld, mrow_ready, mod_used = sem("gpost_ld"), sem("small_ld"), sem("mrow_ready"), sem("mod_used")
        gate_done, modc_ready = sem("gate_done"), sem("modc_ready")
        sq_done, var_ready, rstd_ready, xh_ready = sem("sq_done"), sem("var_ready"), sem("rstd_ready"), sem("xh_ready")
        xhT_ready, modv_ready, acthi, actlo = sem("xhT_ready"), sem("modv_ready"), sem("acthi"), sem("actlo")
        z_act, z_dve = sem("z_act"), sem("z_dve")
        gelu_done, svar_ready, srstd_ready, sv_ready = sem("gelu_done"), sem("svar_ready"), sem("srstd_ready"), sem("sv_ready")
        sgw_T, sgw_ready, sgu_mm, sgu_out = sem("sgw_T"), sem("sgw_ready"), sem("sgu_mm"), sem("sgu_out")
        f1, fU_ready, f2, fY_ready, f3, four_out = (sem(n) for n in ("f1", "fU_ready", "f2", "fY_ready", "f3", "four_out"))
        rope_done, qctx_ready, winT, winT_out = sem("rope_done"), sem("qctx_ready"), sem("winT"), sem("winT_out")
        msq, mvar_ready, mrstd_ready, mxn = sem("msq"), sem("mvar_ready"), sem("mrstd_ready"), sem("mxn")
        mT, mT_out, qkv_mm, qkv_out, mT2, mT2_out = (sem(n) for n in ("mT", "mT_out", "qkv_mm", "qkv_out", "mT2", "mT2_out"))
        scores, smax, probs_ready, probs_T, probT_ready, pv, att_out = (
            sem(n) for n in ("scores", "smax", "probs_ready", "probs_T", "probT_ready", "pv", "att_out"))
        mixT, mix_hi, mix_lo = sem("mixT"), sem("mix_hi"), sem("mix_lo")
        psq, pvar_ready, prstd_ready, h_ready = sem("psq"), sem("pvar_ready"), sem("prstd_ready"), sem("h_ready")
        silu_done, hmul, hth_ready, htl_ready, even_used = (
            sem(n) for n in ("silu_done", "hmul", "hth_ready", "htl_ready", "even_used"))
        wr_hi, wr_ready, logits_mm, top_ready, egap_ready, chosen_ready, rank_mm, rank_ready = (
            sem(n) for n in ("wr_hi", "wr_ready", "logits_mm", "top_ready", "egap_ready", "chosen_ready", "rank_mm", "rank_ready"))
        pick_ready, gather_mm, pickT_mm, pickT_ready, gv_ready, xg_hi_ready, xg_ready = (
            sem(n) for n in ("pick_ready", "gather_mm", "pickT_mm", "pickT_ready", "gv_ready", "xg_hi_ready", "xg_ready"))
        e_silu, e_h, e_T, e_hi, e_lo, ysb_ready, scat_mm, y_added = (
            sem(n) for n in ("e_silu", "e_h", "e_T", "e_hi", "e_lo", "ysb_ready", "scat_mm", "y_added"))
        y_done, fsq, fvar, frstd, fin, stored = (sem(n) for n in ("y_done", "fsq", "fvar", "frstd", "fin", "stored"))
        dve_c, act_c = sem("dve_c"), sem("act_c")
        chain = {"dve": 0, "act": 0}

        def wait(e, s, n):
            if isinstance(n, int) and n <= 0:
                return
            e.wait_ge(s, n)

        raw_before = [U_MOE // NRAW] * NRAW + [0] * (MRAW - NRAW)

        def in_tiles(l, b):
            return NT if l == 0 or b in (1, 2) else LT

        def zdve_count(l, b):
            return sum(1 for ll in range(DEPTH) for bb in range(IN_BLOCKS)
                       if (ll, bb) <= (l, b) and in_tiles(ll, bb) == NT)

        q_base = [0, QTILES[0]]
        s_base = [0, QTILES[0] // 2]
        a_units = [(t, kind, hh) for t in range(NT) for kind in (0, 1) for hh in range(4)]
        att_base = [0, QTILES[0] * 8]

        block = stack.enter_context(nc.Block())


        @block.sync
        def _(sp):
            def load(u, src):
                s = u % NRAW
                wait(sp, lo_done, u - NRAW + 1)
                dst = raw[s][:, 0:int(np.prod(src.shape[1:]))].rearrange("p (a b) -> p a b", a=src.shape[1])
                sp.dma_start(dst, src).then_inc(raw_full[s], 16)

            def halves(w, ncols, b, half):
                return w.rearrange("(c p) n -> p c n", p=P)[:, 4 * half:4 * half + 4, b * ncols:(b + 1) * ncols]

            def program():
                sp.dma_start(rows[R_C:R_C + 8, :], c.rearrange("a (r n) -> (a r) n", n=P)).then_inc(cond_ld, 16)
                sp.dma_start(rows[R_CTX:R_CTX + 8, :], c_ctx.rearrange("(r n) -> r n", n=P)).then_inc(cond_ld, 16)
                sp.dma_start(con[:, :], consts).then_inc(con_ld, 16)
                for l in range(DEPTH):
                    for b in range(MOD_BLOCKS):
                        for half in range(2):
                            load(U_MOD[l] + 2 * b + half, halves(w_mod[l], 512, b, half))
                    for b in range(IN_BLOCKS):
                        for half in range(2):
                            load(U_IN[l] + 2 * b + half, halves(w_in[l], IN_W, b, half))
                    for b in range(2):
                        for half in range(2):
                            load(U_OUT[l] + 2 * b + half, halves(w_out[l], 512, b, half))
                    if l == 0:
                        gate_v, up_v = (w[0].rearrange("(c p) n -> p c n", p=P) for w in (ffn_w_gate, ffn_w_up))
                        down_v = ffn_w_down[0].rearrange("(f p) n -> p f n", p=P)
                        for q in range(FB // 2):
                            load(U_GU + 2 * q, gate_v[:, :, q * 256:(q + 1) * 256])
                            load(U_GU + 2 * q + 1, up_v[:, :, q * 256:(q + 1) * 256])
                        for w in range(N_DN):
                            load(U_DN + w, down_v[:, 2 * w:2 * w + 2, :])
                wait(sp, lo_done, U_MOE)
                wait(sp, h_ready, POST_BASE[(1, 0)] + LT)
                gv_ = moe_w_gate[0].rearrange("e (a c p) n -> e a p c n", p=P, c=4)
                uv_ = moe_w_up[0].rearrange("e (a c p) n -> e a p c n", p=P, c=4)
                dv_ = moe_w_down[0].rearrange("e (f p) n -> e p f n", p=P)

                def eload(k, ee, slot_k, src):
                    wait(sp, lo_done, ee * N_EXP + k + (U_MOE - MRAW + 1))
                    sp.dma_start(raw[slot_k % MRAW][:, :].rearrange("p (a b) -> p a b", a=src.shape[1]),
                                 src).then_inc(raw_full[slot_k % MRAW], 16)

                def expert(e, ee):
                    for half in range(2):
                        eload(half, ee, half, gv_[e, half, :, :, 0:512])
                    for half in range(2):
                        eload(2 + half, ee, 2 + half, uv_[e, half, :, :, 0:512])
                    with sp.Fori(1, EB) as b:
                        cols_b = bass.ds(b * 512, 512)
                        for half in range(2):
                            eload(b * 6 + (half - 2), ee, 4 + half, gv_[e, half, :, :, cols_b])
                        for half in range(2):
                            eload(b * 6 + half, ee, 6 + half, uv_[e, half, :, :, cols_b])
                        for half in range(2):
                            eload(b * 6 + (2 + half), ee, 8 + half, dv_[e, :, bass.ds(b * 4 + (2 * half - 4), 2), :])
                    for half in range(2):
                        eload(40 + half, ee, 40 + half, dv_[e, :, 4 * EB - 4 + 2 * half:4 * EB - 2 + 2 * half, :])

                with sp.Fori(0, NE) as e:
                    expert(e, e + 0)
                sp.wait_ge(rank_ready, 1)
                with sp.Fori(0, MAX_OVER) as i:
                    more = sp.value_load(more_i[0:1, bass.ds(i, 1)], min_val=0, max_val=1)
                    with sp.If(more):
                        e = sp.value_load(more_e[0:1, bass.ds(i, 1)], min_val=0, max_val=NE - 1)
                        expert(e, i + NE)
                    sp.nop()
                sp.wait_ge(fin, LT)
                for t in range(LT):
                    sp.dma_start(out[0, t * P:(t + 1) * P, :], h[:, t, :]).then_inc(stored, 16)
                sp.wait_ge(stored, 16 * LT)

            program()

        @block.gpsimd
        def _(pool):
            def power(dst, src, n, ready, count, done):
                pool.wait_ge(ready, count)
                pool.tensor_tensor(dst, src, mhalf[:, 0:n], ALU.pow).then_inc(done, 1)

            def layer_loads(l):
                if l:
                    pool.wait_ge(h_ready, POST_BASE[(0, 1)] + NT)
                for i in range(QTILES[l] // LT):
                    pool.dma_start(gate_a[:, i, :], g_post_mix[l].partition_broadcast(P)).then_inc(gpost_ld, 16)
                    pool.dma_start(gate_f[:, i, :], g_post_ffn[l].partition_broadcast(P)).then_inc(gpost_ld, 16)
                pool.dma_start(w_uq[:, :, :], mla_w_uq[l].rearrange("(c p) n -> p c n", p=P)).then_inc(small_ld, 16)
                pool.dma_start(w_ukv[:, :], mla_w_ukv[l]).then_inc(small_ld, 16)
                pool.dma_start(w_four[:, :, :], w_fourier[l].rearrange("(c p) n -> p c n", p=P)).then_inc(small_ld, 16)
                pool.dma_start(sgw[:, :, :], sgu_w[l].rearrange("g p q -> p g q")).then_inc(small_ld, 16)
                for b in range(MOD_BLOCKS):
                    gb = l * MOD_BLOCKS + b
                    wait(pool, mod_used, gb - 1)
                    pool.dma_start(mrow[gb % 2][4:5, :], b_mod[l:l + 1, b * 512:(b + 1) * 512]).then_inc(bmod_ld[gb % 2], 16)

            def program():
                for r, src in ((R_PRE_MIX, g_pre_mix), (R_PRE_FFN, g_pre_ffn), (R_GQ, mla_g_q), (R_GKV, mla_g_kv)):
                    v = src.rearrange("l (r n) -> (l r) n", n=P)
                    pool.dma_start(rows[r:r + v.shape[0], :], v).then_inc(rows_ld, 16)
                pool.dma_start(rows[R_SGB:R_SGB + 8, :], sgu_b.rearrange("l g n -> (l g) n")).then_inc(rows_ld, 16)
                for t in range(NT):
                    src = x if t < LT else ctx_in
                    pool.dma_start(h[:, t, :], src[0, (t % LT) * P:(t % LT + 1) * P, :]).then_inc(h_ld, 16)
                pool.dma_start(sinks[:, :], win_sink.rearrange("l h -> (l h)").partition_broadcast(P)).then_inc(sink_ld, 16)
                pool.dma_start(wr[:, :, :], moe_w_router[0].rearrange("(c p) n -> p c n", p=P)).then_inc(wr_ld, 16)
                for l in range(DEPTH):
                    layer_loads(l)
                    power(rstd[:, :], var[:, :], 4, var_ready, NORM_NO[(l, 0)] + 1, rstd_ready)
                    q = QTILES[l]
                    power(srstd[:, 0:q], svar[:, 0:q], q, svar_ready, l + 1, srstd_ready)
                    power(mrstd[:, :, :].rearrange("p a b -> p (a b)"), mvar[:, :, :].rearrange("p a b -> p (a b)"), 8,
                          mvar_ready, l + 1, mrstd_ready)
                    power(prstd[:, 0:q], pvar[:, 0:q], q, pvar_ready, POST_NO[(l, 0)] + 1, prstd_ready)
                    power(rstd[:, 0:q], var[:, 0:q], q, var_ready, NORM_NO[(l, 1)] + 1, rstd_ready)
                    if l == 0:
                        power(prstd[:, :], pvar[:, :], 4, pvar_ready, POST_NO[(0, 1)] + 1, prstd_ready)
                power(prstd[:, 0:2], pvar[:, 0:2], 2, fvar, 1, frstd)

            program()

        @block.scalar
        def _(act):
            def copy(dst, src, **kw):
                return act.activation(dst, src, ACT.Copy, **kw)

            def split_hi(u):
                if u >= U_MOE:
                    return
                act.wait_ge(raw_full[u % NRAW], 16 * (u // NRAW + 1))
                wait(act, unit_used, u - NSPLIT + 1)
                n = 4 * IN_W if U_IN[0] <= u < U_OUT[0] or U_IN[1] <= u < U_OUT[1] else UNIT
                copy(whi[u % NSPLIT][:, 0:n], raw[u % NRAW][:, 0:n]).then_inc(hi_done, 1)

            def norm(l, w):
                n0, nt = NORM_BASE[(l, w)], NORM_TILES[(l, w)]
                if (l, w) == (0, 0):
                    act.wait_ge(h_ld, 16 * NT)
                else:
                    act.wait_ge(h_ready, {(0, 1): 4, (1, 0): 8, (1, 1): 10}[(l, w)])
                for t in range(nt):
                    if t:
                        act.wait_ge(sq_done, n0 + t)
                    act.activation(junk[:, :], h[:, t, :], ACT.Square, accum_out=ss[:, t:t + 1]).then_inc(sq_done, 1)
                for t in range(nt):
                    act.wait_ge(modv_ready, n0 + t + 1)
                    copy(actT[0][:, :, t * P:(t + 1) * P],
                         modv[t % 2][:, :].rearrange("p (c n) -> p c n", c=KC)).then_inc(acthi, 1)

            def in_proj(l):
                for b in range(IN_BLOCKS):
                    for half in range(2):
                        split_hi(U_IN[l] + 2 * b + half + 2)
                    act.wait_ge(unit_used, U_IN[l] + 2 * b + 2)
                    for t in range(LT):
                        ins = copy(z[:, t, b * IN_W:(b + 1) * IN_W], ps[:, (b % 2) * 4 + t, 0:IN_W])
                    ins.then_inc(z_act, 1)

            def mixer(l):
                qt = QTILES[l]
                act.wait_ge(z_dve, zdve_count(l, IN_BLOCKS - 1))
                act.wait_ge(z_act, IN_BLOCKS * (l + 1))
                for t in range(qt):
                    act.activation(z[:, t, C_SG:DIN], z[:, t, C_SG:DIN], ACT.Gelu).then_inc(gelu_done, 1)
                done = l * 2 * NT
                for t in range(NT):
                    if t < qt:
                        wait(act, msq, done)
                        act.activation(mjunk[:, :], z[:, t, C_CQ:C_CKV], ACT.Square,
                                       accum_out=mss[:, t, 0:1]).then_inc(msq, 1)
                        done += 1
                    wait(act, msq, done)
                    done += 1
                    act.activation(mjunk[:, 0:P], z[:, t, C_CKV:C_KR], ACT.Square,
                                   accum_out=mss[:, t, 1:2]).then_inc(msq, 1)
                for s in range(qt // 2):
                    si = s_base[l] + s
                    act.wait_ge(f1, si + 1)
                    wait(act, f2, si)
                    copy(fU[:, :, :], ps[:, 3:5, :]).then_inc(fU_ready, 1)
                    act.wait_ge(f3, si + 1)
                    copy(z[:, 2 * s:2 * s + 2, 0:GW], ps[:, 6, :].rearrange("p (k n) -> p k n", k=2)).then_inc(four_out, 1)
                for t in range(NT):
                    b = 1 + t % 2
                    act.wait_ge(winT, l * NT + t + 1)
                    if t < qt:
                        copy(qTw[:, :, t * P:(t + 1) * P], ps[:, b, 0:256].rearrange("p (a n) -> p a n", a=2),
                             scale=HD ** -0.5)
                    copy(kTw[:, t * P:(t + 1) * P], ps[:, b, 256:384]).then_inc(winT_out, 1)
                for i in range(NT + 2):
                    if i < NT:
                        t = i
                        b = 3 + t % 2
                        act.wait_ge(mT, l * NT + t + 1)
                        if t < qt:
                            for j in range(2):
                                copy(cqT[:, j, t * P:(t + 1) * P], ps[:, b, j * P:(j + 1) * P],
                                     scale=cols[:, R_GQ + 2 * l + j:R_GQ + 2 * l + j + 1])
                        copy(ckvT[:, t * P:(t + 1) * P], ps[:, b, 256:384],
                             scale=cols[:, R_GKV + l:R_GKV + l + 1]).then_inc(mT_out, 1)
                    if i >= 2:
                        t = i - 2
                        act.wait_ge(mT2, l * NT + t + 1)
                        if t < qt:
                            copy(qTm[0:QK, :, t * P:(t + 1) * P], ps[0:QK, 7, :].rearrange("p (a n) -> p a n", a=4),
                                 scale=QK ** -0.5)
                        copy(kTm[0:QK, :, t * P:(t + 1) * P],
                             ps[0:QK, 0, :].rearrange("p (a n) -> p a n", a=4)).then_inc(mT2_out, 1)
                n = qt * 8
                for i in range(n + 1):
                    if i < n:
                        t, kind, hh = a_units[i]
                        g = att_base[l] + i
                        nk = NT if t < LT else NT - LT
                        act.wait_ge(smax, g + 1)
                        wait(act, probs_T, g - 1)
                        wait(act, att_out, g - 1)
                        if kind == 0:
                            act.activation(esink[:, i % 2:i % 2 + 1], sinks[:, l * WH + hh:l * WH + hh + 1], ACT.Exp,
                                           bias=nmax[:, i % 2:i % 2 + 1])
                        act.activation(probs[i % 2][:, 0:nk * P], ps[:, i % 2, 0:nk * P], ACT.Exp,
                                       bias=nmax[:, i % 2:i % 2 + 1],
                                       accum_out=rsum[:, i % 2:i % 2 + 1]).then_inc(probs_ready, 1)
                    if i >= 1:
                        j = i - 1
                        g = att_base[l] + j
                        nk = NT if a_units[j][0] < LT else NT - LT
                        act.wait_ge(probs_T, g + 1)
                        wait(act, pv, g - 1)
                        copy(probT[j % 2][:, 0:nk * P], ps[:, 2 + j % 2, 0:nk * P]).then_inc(probT_ready, 1)

            def post(l, w, used):
                act.wait_ge(unit_used, used)
                for t in range(POST_TILES[(l, w)]):
                    for hf in range(2):
                        wait(act, psq, 2 * (POST_BASE[(l, w)] + t) + hf - 1)
                        act.activation(junk[:, hf * 512:(hf + 1) * 512], ps[:, hf * 4 + t, :], ACT.Square,
                                       accum_out=pss[:, t, hf:hf + 1]).then_inc(psq, 1)

            def out_proj(l):
                qt = QTILES[l]
                for t in range(qt):
                    b = 2 * (t % 2)
                    act.wait_ge(mixT, q_base[l] + t + 1)
                    copy(actT[0][:, :, t * P:(t + 1) * P],
                         ps[:, b:b + 2, :].rearrange("p a (c n) -> p (a c) n", c=4)).then_inc(mix_hi, 1)
                for k in range(N_OUT):
                    split_hi(U_OUT[l] + k + 2)
                post(l, 0, U_OUT[l] + N_OUT)

            def ffn():
                for q in range(FB // 2):
                    u = U_GU + 2 * q
                    split_hi(u + 2)
                    act.wait_ge(unit_used, u + 1)
                    wait(act, hmul, q - 1)
                    b = (q % 2) * 4
                    act.activation(sgate[q % 2][:, :, :], ps[:, b:b + 2, :], ACT.Silu).then_inc(silu_done, 1)
                    split_hi(u + 3)

                def upper(f):
                    if f % 2 == 0:
                        wait(act, even_used, f // 2)
                    else:
                        wait(act, unit_used, U_DN + f // 2)
                    copy(hth[f % 2][:, :], hT[f][:, :]).then_inc(hth_ready, 1)

                act.wait_ge(hmul, FB // 2)
                for w in range(N_DN):
                    upper(2 * w)
                    split_hi(U_DN + w + 2)
                    upper(2 * w + 1)
                post(0, 1, U_DN + N_DN)

            def expert(e, ee):
                def esplit(k, slot_k, extra):
                    s = slot_k % MRAW
                    act.wait_ge(raw_full[s], ee * (16 * 7) + extra + 16 * (raw_before[s] + slot_k // MRAW))
                    act.wait_ge(unit_used, ee * N_EXP + k + (U_MOE - NSPLIT + 1))
                    copy(whi[slot_k % NSPLIT][:, :], raw[s][:, :]).then_inc(hi_done, 1)

                def silu(units, hs):
                    act.wait_ge(unit_used, units)
                    act.wait_ge(e_h, hs)
                    act.activation(esg[:, :], ps[:, 0, :], ACT.Silu).then_inc(e_silu, 1)

                def upper(Ts):
                    act.wait_ge(e_T, Ts)
                    copy(ehT[0][:, :, :], ps[:, 2, :].rearrange("p (a n) -> p a n", a=4)).then_inc(e_hi, 1)

                esplit(0, 0, 16)
                esplit(1, 1, 16)
                act.wait_ge(gv_ready, ee + 1)
                copy(xg[0][:, :, :], gv[:, :, :]).then_inc(xg_hi_ready, 1)
                esplit(2, 2, 16)
                esplit(3, 3, 16)
                silu(ee * N_EXP + (U_MOE + 2), ee * EB)
                esplit(4, 4, 16)
                esplit(5, 5, 16)
                with act.Fori(1, EB) as b:
                    esplit(b * 6, 6, b * 16)
                    esplit(b * 6 + 1, 7, b * 16)
                    silu(ee * N_EXP + b * 6 + U_MOE, ee * EB + b)
                    upper(ee * EB + b)
                    for j in range(2, 6):
                        esplit(b * 6 + j, 6 + j, b * 16)
                upper(ee * EB + EB)
                act.wait_ge(unit_used, ee * N_EXP + (U_MOE + N_EXP))
                act.wait_ge(scat_mm, ee)
                copy(ysb[:, :], ps[:, 5:7, :].rearrange("p a n -> p (a n)")).then_inc(ysb_ready, 1)

            def program():
                act.wait_ge(cols_ready, 1)
                act.activation(condf[:, :], cols[:, 0:2 * KC], ACT.Silu).then_inc(silu_c, 1)
                for u in range(2):
                    split_hi(u)
                for l in range(DEPTH):
                    for k in range(N_MOD):
                        split_hi(U_MOD[l] + k + 2)
                    norm(l, 0)
                    in_proj(l)
                    mixer(l)
                    out_proj(l)
                    norm(l, 1)
                    if l == 0:
                        ffn()
                act.wait_ge(wr_ld, 16)
                copy(wrh[:, :, :], wr[:, :, :]).then_inc(wr_hi, 1)
                act.wait_ge(top_ready, 1)
                act.activation(egap[:, :], gap[:, :], ACT.Exp).then_inc(egap_ready, 1)
                with act.Fori(0, NE) as e:
                    expert(e, e + 0)
                act.wait_ge(rank_ready, 1)
                with act.Fori(0, MAX_OVER) as i:
                    more = act.value_load(more_i[0:1, bass.ds(i, 1)], min_val=0, max_val=1)
                    with act.If(more):
                        e = act.value_load(more_e[0:1, bass.ds(i, 1)], min_val=0, max_val=NE - 1)
                        expert(e, i + NE)
                    act.nop()
                act.wait_ge(y_done, 1)
                for t in range(LT):
                    wait(act, fsq, t)
                    act.activation(gv[:, :, :].rearrange("p a n -> p (a n)"), y[:, t, :], ACT.Square,
                                   accum_out=pss[:, t, 0:1]).then_inc(fsq, 1)

            program()

        @block.tensor
        def _(pe):
            def mm(o, lhsT, rhs, start=True, stop=True):
                return pe.matmul(o, lhsT, rhs, start=start, stop=stop)

            def mm3(o, a, b, start, stop):
                mm(o, a[0], b[0], start, False)
                mm(o, a[0], b[1], False, False)
                return mm(o, a[1], b[0], False, stop)

            def piece(u):
                pe.wait_ge(lo_done, u + 1)
                return whi[u % NSPLIT], wlo[u % NSPLIT]

            def mod_rows(l, b):
                gb = l * MOD_BLOCKS + b
                wait(pe, mrow_ready, gb - 1)
                for half in range(2):
                    w2 = piece(U_MOD[l] + 2 * b + half)
                    for k in range(4):
                        for i in range(2):
                            ins = mm(ps[:, gb % 2, :], cond4[:, 4 * half + k, :], w2[i][:, k * 512:(k + 1) * 512],
                                     start=half + k + i == 0, stop=half == 1 and k == 3 and i == 1)
                    ins.then_inc(unit_used, 1)

            def mod_spread(l, b):
                gb = l * MOD_BLOCKS + b
                pe.wait_ge(mrow_ready, gb + 1)
                pe.wait_ge(bmod_ld[gb % 2], 16 * (gb // 2 + 1))
                m = mrow[gb % 2]
                if b // 2 in (2, 5):
                    wait(pe, gate_done, gate_no(l, b))
                    for i in range(QTILES[l] // LT):
                        ins = mm(ps[:, 3 + i, :], selrow[0:5, i, :], m[0:5, :])
                else:
                    for j in range(4):
                        at_ = ((b // 2) * KC + (b % 2) * 4 + j) * 2
                        ins = mm(ps[:, 2, at_:at_ + 2], m[0:5, j * P:(j + 1) * P], K("selcol")[0:5, :])
                ins.then_inc(mod_used, 1)

            def norm(l, w):
                n0 = NORM_BASE[(l, w)]
                if w == 0:
                    pe.wait_ge(modc_ready, l + 1)
                for t in range(NORM_TILES[(l, w)]):
                    pe.wait_ge(xh_ready, n0 + t + 1)
                    if t >= 2:
                        pe.wait_ge(modv_ready, n0 + t - 1)
                    for k in range(KC):
                        b = 2 * (t % 2) + k // 4
                        ins = pe.transpose(ps[:, b, (k % 4) * P:(k % 4 + 1) * P], xh[t % 2][:, k * P:(k + 1) * P], ident)
                    ins.then_inc(xhT_ready, 1)

            def in_proj(l):
                pe.wait_ge(actlo, NORM_BASE[(l, 0)] + NT)
                for b in range(IN_BLOCKS):
                    for half in range(2):
                        w2 = piece(U_IN[l] + 2 * b + half)
                        if half == 0 and b >= 2:
                            pe.wait_ge(z_act, l * IN_BLOCKS + b - 1)
                            pe.wait_ge(z_dve, zdve_count(l, b - 2))
                        for t in range(in_tiles(l, b)):
                            for k in range(4):
                                a = [x_[:, 4 * half + k, t * P:(t + 1) * P] for x_ in actT]
                                ins = mm3(ps[:, (b % 2) * 4 + t, 0:IN_W], a, [w_[:, k * IN_W:(k + 1) * IN_W] for w_ in w2],
                                          half + k == 0, half == 1 and k == 3)
                        ins.then_inc(unit_used, 1)

            def mixer(l):
                qt = QTILES[l]
                pe.wait_ge(z_act, IN_BLOCKS * (l + 1))
                pe.wait_ge(z_dve, zdve_count(l, IN_BLOCKS - 1))
                pe.wait_ge(small_ld, 16 * 4 * (l + 1))
                for g in range(4):
                    ins = pe.transpose(ps[:, 0, g * P:(g + 1) * P], sgw[:, g, :], ident)
                ins.then_inc(sgw_T, 1)
                pe.wait_ge(sgw_ready, l + 1)
                for t in range(qt):
                    pe.wait_ge(sv_ready, q_base[l] + t + 1)
                    wait(pe, sgu_out, q_base[l] + t - 1)
                    for g in range(4):
                        ins = mm(ps[:, 1 + t % 2, g * 64:(g + 1) * 64], sgwT[:, g, :],
                                 z[:, t, C_SG + GW + g * 64:C_SG + GW + (g + 1) * 64])
                    ins.then_inc(sgu_mm, 1)
                for s in range(qt // 2):
                    si = s_base[l] + s
                    wait(pe, fU_ready, si)
                    for m in range(2):
                        for k in range(2):
                            ins = mm(ps[:, 3 + m, :], z[:, 2 * s + k, m * P:(m + 1) * P], dft[:, k, :], k == 0, k == 1)
                    ins.then_inc(f1, 1)
                    pe.wait_ge(fU_ready, si + 1)
                    for m in range(2):
                        o = ps[:, 5, m * 256:(m + 1) * 256]
                        mm(o, K("cch"), fU[:, m, 0:256], True, False)
                        ins = mm(o, K("nsch"), fU[:, m, 256:512], False, True)
                    ins.then_inc(f2, 1)
                    pe.wait_ge(fY_ready, si + 1)
                    wait(pe, four_out, si)
                    for k in range(2):
                        for m in range(2):
                            ins = mm(ps[:, 6, k * 256:(k + 1) * 256], fY[:, m, k * P:(k + 1) * P], w_four[:, m, :],
                                     m == 0, m == 1)
                    ins.then_inc(f3, 1)
                pe.wait_ge(rope_done, 2 * (l + 1))
                if l == 0:
                    pe.wait_ge(qctx_ready, NT - LT)
                pe.wait_ge(sgu_out, q_base[l] + qt)
                for t in range(NT):
                    b = 1 + t % 2
                    if t >= 2:
                        pe.wait_ge(winT_out, l * NT + t - 1)
                    q_ = qkr[:, t, 0:256] if t < LT else qctx[:, t - LT, :]
                    k_ = qkr[:, t, 256:384] if t < LT else z[:, t, C_WK:C_WV]
                    if t < qt:
                        for j in range(2):
                            pe.transpose(ps[:, b, j * P:(j + 1) * P], q_[:, j * P:(j + 1) * P], ident)
                    pe.transpose(ps[:, b, 256:384], k_, ident).then_inc(winT, 1)
                for i in range(NT + 2):
                    if i < NT:
                        t = i
                        b = 3 + t % 2
                        pe.wait_ge(mxn, l * NT + t + 1)
                        if t >= 2:
                            pe.wait_ge(mT_out, l * NT + t - 1)
                        if t < qt:
                            for j in range(2):
                                pe.transpose(ps[:, b, j * P:(j + 1) * P], z[:, t, C_CQ + j * P:C_CQ + (j + 1) * P], ident)
                        pe.transpose(ps[:, b, 256:384], z[:, t, C_CKV:C_KR], ident).then_inc(mT, 1)
                    if 1 <= i <= NT:
                        t = i - 1
                        pe.wait_ge(mT_out, l * NT + t + 1)
                        if t == 0:
                            pe.wait_ge(four_out, s_base[l] + qt // 2)
                        else:
                            pe.wait_ge(qkv_out, l * NT + t)
                        if t < qt:
                            for j in range(2):
                                mm(ps[:, 5, 0:384], cqT[:, j, t * P:(t + 1) * P], w_uq[:, j, :], j == 0, j == 1)
                        mm(ps[:, 6, :], ckvT[:, t * P:(t + 1) * P], w_ukv[:, :]).then_inc(qkv_mm, 1)
                    if i >= 2:
                        t = i - 2
                        pe.wait_ge(qkv_out, l * NT + t + 1)
                        if t:
                            pe.wait_ge(mT2_out, l * NT + t)
                        for hh in range(MH):
                            if t < qt:
                                pe.transpose(ps[0:QK, 7, hh * P:(hh + 1) * P], qm[t % 2][:, hh, :], ident)
                            ins = pe.transpose(ps[0:QK, 0, hh * P:(hh + 1) * P], km[t % 2][:, hh, :], ident)
                        ins.then_inc(mT2, 1)
                pe.wait_ge(winT_out, NT * (l + 1))
                pe.wait_ge(mT2_out, NT * (l + 1))
                n = qt * 8
                for i in range(n + 2):
                    if i < n:
                        t, kind, hh = a_units[i]
                        g = att_base[l] + i
                        k0 = 0 if t < LT else LT
                        wait(pe, probs_ready, g - 1)
                        if kind == 0:
                            pr = slice(64 * (hh // 2), 64 * (hh // 2) + 64)
                            mm(ps[:, i % 2, 0:(NT - k0) * P], qTw[pr, hh % 2, t * P:(t + 1) * P],
                               kTw[pr, k0 * P:]).then_inc(scores, 1)
                        else:
                            mm(ps[:, i % 2, 0:(NT - k0) * P], qTm[0:QK, hh, t * P:(t + 1) * P],
                               kTm[0:QK, hh, k0 * P:]).then_inc(scores, 1)
                    if 1 <= i <= n:
                        j = i - 1
                        g = att_base[l] + j
                        nk = NT if a_units[j][0] < LT else NT - LT
                        pe.wait_ge(probs_ready, g + 1)
                        wait(pe, probT_ready, g - 1)
                        for k in range(nk):
                            ins = pe.transpose(ps[:, 2 + j % 2, k * P:(k + 1) * P], probs[j % 2][:, k * P:(k + 1) * P], ident)
                        ins.then_inc(probs_T, 1)
                    if i >= 2:
                        j = i - 2
                        t, kind, hh = a_units[j]
                        g = att_base[l] + j
                        k0 = 0 if t < LT else LT
                        pe.wait_ge(probT_ready, g + 1)
                        wait(pe, att_out, g - 1)
                        for k in range(k0, NT):
                            v = z[:, k, C_WV + (hh // 2) * HD:C_WV + (hh // 2 + 1) * HD] if kind == 0 else \
                                vm[:, k, hh * HD:(hh + 1) * HD]
                            ins = mm(ps[:, 4 + j % 2, 0:HD], probT[j % 2][:, (k - k0) * P:(k - k0 + 1) * P], v,
                                     k == k0, k == NT - 1)
                        ins.then_inc(pv, 1)

            def out_proj(l):
                qt = QTILES[l]
                pe.wait_ge(att_out, att_base[l] + 8 * qt)
                pe.wait_ge(sgu_out, q_base[l] + qt)
                pe.wait_ge(four_out, s_base[l] + qt // 2)
                for t in range(qt):
                    if t >= 2:
                        pe.wait_ge(mix_lo, q_base[l] + t - 1)
                    for k in range(KC):
                        b = 2 * (t % 2) + k // 4
                        ins = pe.transpose(ps[:, b, (k % 4) * P:(k % 4 + 1) * P],
                                           z[:, t, MIX_COLS[k]:MIX_COLS[k] + P], ident)
                    ins.then_inc(mixT, 1)
                pe.wait_ge(mix_lo, q_base[l] + qt)
                for b in range(2):
                    for half in range(2):
                        w2 = piece(U_OUT[l] + 2 * b + half)
                        for t in range(qt):
                            for k in range(4):
                                a = [x_[:, 4 * half + k, t * P:(t + 1) * P] for x_ in actT]
                                ins = mm3(ps[:, b * 4 + t, :], a, [w_[:, k * 512:(k + 1) * 512] for w_ in w2],
                                          half + k == 0, half == 1 and k == 3)
                        ins.then_inc(unit_used, 1)

            def ffn():
                pe.wait_ge(actlo, NORM_BASE[(0, 1)] + NT)
                for q in range(FB // 2):
                    for i in range(2):
                        w2 = piece(U_GU + 2 * q + i)
                        if q >= 2:
                            pe.wait_ge((silu_done, hmul)[i], q - 1)
                        for j in range(2):
                            for k in range(KC):
                                a = [w_[:, k * 256 + j * P:k * 256 + (j + 1) * P] for w_ in w2]
                                ins = mm3(ps[:, (q % 2) * 4 + 2 * i + j, :], a, [x_[:, k, :] for x_ in actT],
                                          k == 0, k == KC - 1)
                        ins.then_inc(unit_used, 1)
                pe.wait_ge(hmul, FB // 2)
                for w in range(N_DN):
                    w2 = piece(U_DN + w)
                    for i in range(2):
                        f = 2 * w + i
                        pe.wait_ge(htl_ready, f + 1)
                        for t in range(NT):
                            for hf in range(2):
                                a = [hth[f % 2][:, t * P:(t + 1) * P], htl[f % 2][:, t * P:(t + 1) * P]]
                                ins = mm3(ps[:, hf * 4 + t, :], a,
                                          [w_[:, i * D + hf * 512:i * D + (hf + 1) * 512] for w_ in w2], f == 0, f == FB - 1)
                        ins.then_inc((even_used, unit_used)[i], 1)

            def router():
                pe.wait_ge(actlo, NORM_BASE[(1, 1)] + LT)
                pe.wait_ge(wr_ready, 1)
                for t in range(LT):
                    for k in range(KC):
                        for i in range(2):
                            for j in range(2):
                                ins = mm(ps[:, 4, t * NE:(t + 1) * NE], actT[i][:, k, t * P:(t + 1) * P],
                                         (wrh, wrl)[j][:, k, :], k + i + j == 0, k == KC - 1 and i + j == 2)
                ins.then_inc(logits_mm, 1)
                pe.wait_ge(chosen_ready, 1)
                mm(ps[:, 5, 0:NE], K("before"), chosen[:, 0, :])
                mm(ps[:, 5, NE:2 * NE], K("before"), chosen[:, 1, :], True, False)
                mm(ps[:, 5, NE:2 * NE], K("ones"), chosen[:, 0, :], False, True)
                mm(ps[:, 5, 2 * NE:3 * NE], K("ones"), chosen[:, 0, :], True, False)
                mm(ps[:, 5, 2 * NE:3 * NE], K("ones"), chosen[:, 1, :], False, True).then_inc(rank_mm, 1)

            def expert(e, ee):
                def gate_up(us, slot_k, bank, sm, count):
                    for half in range(2):
                        pe.wait_ge(lo_done, us + (half + 1))
                        if half == 0:
                            pe.wait_ge(sm, count)
                        s = (slot_k + half) % NSPLIT
                        for k in range(4):
                            ins = mm3(ps[:, bank, :], [g_[:, 4 * half + k, :] for g_ in xg],
                                      [w_[s][:, k * 512:(k + 1) * 512] for w_ in (whi, wlo)],
                                      half + k == 0, half == 1 and k == 3)
                        ins.then_inc(unit_used, 1)

                def turn(count):
                    pe.wait_ge(e_h, count)
                    pe.wait_ge(e_lo, count - 1)
                    for k in range(4):
                        ins = pe.transpose(ps[:, 2, k * P:(k + 1) * P], eh[:, k * P:(k + 1) * P], ident)
                    ins.then_inc(e_T, 1)

                def down(us, slot_k, count, start, stop):
                    pe.wait_ge(e_lo, count)
                    for half in range(2):
                        pe.wait_ge(lo_done, us + (half + 1))
                        s = (slot_k + half) % NSPLIT
                        for k in range(2):
                            for hf in range(2):
                                ins = mm3(ps[:, 5 + hf, :], [h_[:, 2 * half + k, :] for h_ in ehT],
                                          [w_[s][:, k * D + hf * 512:k * D + (hf + 1) * 512] for w_ in (whi, wlo)],
                                          start and half + k == 0, stop and half + k == 2)
                        ins.then_inc(unit_used, 1)

                pe.wait_ge(pick_ready, ee + 1)
                pe.wait_ge(y_added, ee)
                for k in range(KC):
                    for t in range(LT):
                        ins = mm(ps[:, 3 + k // 4, (k % 4) * P:(k % 4 + 1) * P], xh[t][:, k * P:(k + 1) * P],
                                 pick[:, t, :], t == 0, t == LT - 1)
                ins.then_inc(gather_mm, 1)
                pe.wait_ge(e_silu, ee * EB)
                for t in range(LT):
                    ins = pe.transpose(ps[:, 0, t * P:(t + 1) * P], pick[:, t, :], ident)
                ins.then_inc(pickT_mm, 1)
                pe.wait_ge(pickT_ready, ee + 1)
                pe.wait_ge(xg_ready, ee + 1)
                base = ee * N_EXP + U_MOE
                gate_up(base, 0, 0, e_silu, ee * EB)
                gate_up(base + 2, 2, 1, e_h, ee * EB)
                pe.wait_ge(ysb_ready, ee)
                blocks = [(1, None), (2, None)]
                del blocks

                def step(b, start):
                    gate_up(base + (b * 6 - 2), 4, 0, e_silu, ee * EB + b)
                    turn(ee * EB + b)
                    gate_up(base + b * 6, 6, 1, e_h, ee * EB + b)
                    down(base + (b * 6 + 2), 8, ee * EB + b, start, False)

                step(1, True)
                with pe.Fori(2, EB) as b:
                    step(b, False)
                turn(ee * EB + EB)
                down(base + (N_EXP - 2), 40, ee * EB + EB, False, True)
                pe.wait_ge(ysb_ready, ee + 1)
                for t in range(LT):
                    for hf in range(2):
                        ins = mm(ps[:, SCAT[2 * t + hf], :], pickT[:, t, :], ysb[:, hf * 512:(hf + 1) * 512])
                ins.then_inc(scat_mm, 1)

            def program():
                pe.wait_ge(con_ld, 16)
                pe.wait_ge(cond_ld, 32)
                pe.wait_ge(rows_ld, 16 * 5)
                pe.transpose(ps[:, 0, 0:NROWS], rows[0:NROWS, :], ident[0:NROWS, 0:NROWS]).then_inc(rows_T, 1)
                for l in range(DEPTH):
                    pe.wait_ge(cond_ready, l + 1)
                    if l:
                        pe.wait_ge(h_ready, POST_BASE[(1, 0)])
                    for b in range(MOD_BLOCKS + 1):
                        if b < MOD_BLOCKS:
                            mod_rows(l, b)
                        if b:
                            mod_spread(l, b - 1)
                    norm(l, 0)
                    in_proj(l)
                    mixer(l)
                    out_proj(l)
                    norm(l, 1)
                    if l == 0:
                        ffn()
                router()
                with pe.Fori(0, NE) as e:
                    expert(e, e + 0)
                pe.wait_ge(rank_ready, 1)
                with pe.Fori(0, MAX_OVER) as i:
                    more = pe.value_load(more_i[0:1, bass.ds(i, 1)], min_val=0, max_val=1)
                    with pe.If(more):
                        e = pe.value_load(more_e[0:1, bass.ds(i, 1)], min_val=0, max_val=NE - 1)
                        expert(e, i + NE)
                    pe.nop()

            program()

        @block.vector
        def _(dve):
            chain = [0]

            def link(ins):
                chain[0] += 1
                ins.then_inc(dve_c, 1)
                dve.wait_ge(dve_c, chain[0])

            def split_lo(u):
                if u >= U_MOE:
                    return
                n = 4 * IN_W if U_IN[0] <= u < U_OUT[0] or U_IN[1] <= u < U_OUT[1] else UNIT
                dve.wait_ge(hi_done, u + 1)
                sub(wlo[u % NSPLIT][:, 0:n], raw[u % NRAW][:, 0:n], whi[u % NSPLIT][:, 0:n]).then_inc(lo_done, 1)

            def sub(o, a, b):
                return dve.tensor_tensor(o, a, b.bitcast(F32), ALU.subtract)

            def mod(l):
                cf = condf[:, :].rearrange("p (s c) -> p c s", s=2)
                link(dve.memset(cond4[:, :, :].bitcast(F32), 0.0))
                link(dve.tensor_copy(cond4[:, :, 0:2], cf))
                sub(cond4[:, :, 2:4], cf, cond4[:, :, 0:2]).then_inc(cond_ready, 1)
                for b in range(MOD_BLOCKS + 1):
                    gb = l * MOD_BLOCKS + b
                    if b < MOD_BLOCKS:
                        split_lo(U_MOD[l] + 2 * b + 2)
                        split_lo(U_MOD[l] + 2 * b + 3)
                        dve.wait_ge(unit_used, U_MOD[l] + 2 * b + 2)
                        wait(dve, mod_used, gb - 1)
                        dve.tensor_copy(mrow[gb % 2][0:4, :], ps[0:4, gb % 2, :]).then_inc(mrow_ready, 1)
                    if b and (b - 1) // 2 in (2, 5):
                        gate = gate_a if (b - 1) // 2 == 2 else gate_f
                        cs = slice(((b - 1) % 2) * 512, ((b - 1) % 2 + 1) * 512)
                        dve.wait_ge(gpost_ld, 16 * (4 if l == 0 else 6))
                        dve.wait_ge(mod_used, gb)
                        for i in range(QTILES[l] // LT):
                            ins = dve.tensor_tensor(gate[:, i, cs], ps[:, 3 + i, :], gate[:, i, cs], ALU.mult)
                        ins.then_inc(gate_done, 1)
                dve.wait_ge(mod_used, (l + 1) * MOD_BLOCKS)
                mc = ps[:, 2, 0:96].rearrange("p (v k i) -> p v i k", v=6, i=2)
                for w in range(2):
                    for i in range(2):
                        r = (R_PRE_MIX, R_PRE_FFN)[w] + l * KC
                        dve.scalar_tensor_tensor(out=acol[:, w, i, :], in0=mc[:, 3 * w + 1, i, :], scalar=1.0,
                                                 in1=cols[:, r:r + KC], op0=ALU.add, op1=ALU.mult)
                        ins = dve.tensor_copy(bcol[:, w, i, :], mc[:, 3 * w, i, :])
                ins.then_inc(modc_ready, 1)
                dve.wait_ge(modc_ready, l + 1)

            def modulated(dst, src, w, i):
                for k in range(KC):
                    ins = dve.tensor_scalar(dst[:, k * P:(k + 1) * P], src[:, k, :], acol[:, w, i, k:k + 1],
                                            bcol[:, w, i, k:k + 1], ALU.mult, ALU.add)
                return ins

            def norm(l, w):
                n0, nt, no = NORM_BASE[(l, w)], NORM_TILES[(l, w)], NORM_NO[(l, w)]
                dve.wait_ge(sq_done, n0 + nt)
                dve.tensor_scalar(var[:, 0:nt], ss[:, 0:nt], 1.0 / D, EPS, ALU.mult, ALU.add).then_inc(var_ready, 1)
                dve.wait_ge(rstd_ready, no + 1)
                for t in range(nt + 1):
                    if t < nt:
                        if t >= 2:
                            dve.wait_ge(xhT_ready, n0 + t - 1)
                        dve.tensor_scalar(xh[t % 2][:, :], h[:, t, :], rstd[:, t:t + 1], None, ALU.mult).then_inc(xh_ready, 1)
                    if t:
                        s = t - 1
                        dve.wait_ge(xhT_ready, n0 + s + 1)
                        b = 2 * (s % 2)
                        modulated(modv[s % 2], ps[:, b:b + 2, :].rearrange("p a (c n) -> p (a c) n", c=4), w,
                                  s // LT).then_inc(modv_ready, 1)
                        dve.wait_ge(acthi, n0 + s + 1)
                        hi = actT[0][:, :, s * P:(s + 1) * P]
                        sub(actT[1][:, :, s * P:(s + 1) * P], modv[s % 2][:, :].rearrange("p (c n) -> p c n", c=KC),
                            hi).then_inc(actlo, 1)

            def in_proj(l):
                for b in range(IN_BLOCKS):
                    for half in range(2):
                        split_lo(U_IN[l] + 2 * b + half + 2)
                    if in_tiles(l, b) == NT:
                        dve.wait_ge(unit_used, U_IN[l] + 2 * b + 2)
                        for t in range(LT, NT):
                            ins = dve.tensor_copy(z[:, t, b * IN_W:(b + 1) * IN_W], ps[:, (b % 2) * 4 + t, 0:IN_W])
                        ins.then_inc(z_dve, 1)

            def turn(xe, xo, cs, sn, s4):
                dve.tensor_tensor(s4[0], xe, cs, ALU.mult)
                dve.tensor_tensor(s4[1], xo, sn, ALU.mult)
                dve.tensor_tensor(s4[2], xe, sn, ALU.mult)
                link(dve.tensor_tensor(s4[3], xo, cs, ALU.mult))

            def rotate(oe, oo, xe, xo, cs, sn, s4):
                turn(xe, xo, cs, sn, s4)
                dve.tensor_tensor(oe, s4[0], s4[1], ALU.subtract)
                return dve.tensor_tensor(oo, s4[2], s4[3], ALU.add)

            def pairs(ap, heads, n):
                v = ap.rearrange("p (h n i) -> p i h n", h=heads, i=2)
                return v[:, 0, :, :], v[:, 1, :, :]

            def scratch(heads, n):
                return [s_[:, 0:heads * n].rearrange("p (h n) -> p h n", h=heads) for s_ in rope_s]

            def table(name, t, n, heads):
                return rot(name, t, n).unsqueeze(1).broadcast_to([P, heads, n])

            def mixer(l):
                qt = QTILES[l]
                dve.wait_ge(z_act, IN_BLOCKS * (l + 1))
                dve.wait_ge(z_dve, zdve_count(l, IN_BLOCKS - 1))
                for t in range(LT):
                    xe, xo = pairs(z[:, t, C_WQ:C_WV], 6, 32)
                    turn(xe, xo, table("cosw", t, 32, 6), table("sinw", t, 32, 6), scratch(6, 32))
                    for i, op in ((0, ALU.subtract), (1, ALU.add)):
                        s_ = [r_[:, 0:128].rearrange("p (a b n) -> p a b n", a=2, b=2) for r_ in rope_s[2 * i:2 * i + 2]]
                        o = qkr[:, t, 0:256].rearrange("p (b a n i) -> p i a b n", a=2, b=2, i=2)[:, i, :, :, :]
                        dve.tensor_tensor(o, s_[0], s_[1], op)
                        s_ = [r_[:, 128:192].rearrange("p (h n) -> p h n", h=2) for r_ in rope_s[2 * i:2 * i + 2]]
                        ins = dve.tensor_tensor(pairs(qkr[:, t, 256:384], 2, 32)[i], s_[0], s_[1], op)
                    link(ins)
                    xe, xo = pairs(z[:, t, C_KR:C_SG], 1, 16)
                    oe, oo = pairs(krr[:, t, :], 1, 16)
                    ins = rotate(oe, oo, xe, xo, table("cosm", t, 16, 1), table("sinm", t, 16, 1), scratch(1, 16))
                    link(ins)
                    dve.engine_nop().then_inc(rope_done, 1)
                for t in range(LT, qt):
                    dve.tensor_copy(qctx[:, t - LT, :].rearrange("p (b a n) -> p a b n", a=2, b=2),
                                    z[:, t, C_WQ:C_WK].rearrange("p (a b n) -> p a b n", a=2, b=2)).then_inc(qctx_ready, 1)
                dve.wait_ge(sgw_T, l + 1)
                dve.tensor_copy(sgwT[:, :, :], ps[:, 0, :].rearrange("p (g q) -> p g q", g=4)).then_inc(sgw_ready, 1)
                dve.wait_ge(gelu_done, q_base[l] + qt)
                for t in range(qt):
                    ins = dve.bn_stats(bst[:, t, :], z[:, t, C_SG + GW:DIN])
                link(ins)
                for t in range(qt):
                    ins = dve.bn_aggr(mv[:, t, :], bst[:, t, :])
                link(ins)
                dve.tensor_scalar(svar[:, 0:qt], mv[:, 0:qt, 1], EPS, None, ALU.add).then_inc(svar_ready, 1)
                dve.wait_ge(msq, (2 * NT, 2 * NT + NT + LT)[l])
                dve.tensor_scalar(mvar[:, :, 0], mss[:, :, 0], 1.0 / 256, EPS, ALU.mult, ALU.add)
                dve.tensor_scalar(mvar[:, :, 1], mss[:, :, 1], 1.0 / 128, EPS, ALU.mult, ALU.add).then_inc(mvar_ready, 1)
                dve.wait_ge(srstd_ready, l + 1)
                for t in range(qt):
                    v = z[:, t, C_SG + GW:DIN]
                    dve.tensor_scalar(v, v, mv[:, t, 0:1], srstd[:, t:t + 1], ALU.subtract, ALU.mult).then_inc(sv_ready, 1)
                for t in range(qt):
                    dve.wait_ge(sgu_mm, q_base[l] + t + 1)
                    for g in range(4):
                        u = z[:, t, C_SG + g * 64:C_SG + (g + 1) * 64]
                        r = R_SGB + 4 * l + g
                        ins = dve.scalar_tensor_tensor(out=u, in0=ps[:, 1 + t % 2, g * 64:(g + 1) * 64],
                                                       scalar=cols[:, r:r + 1], in1=u, op0=ALU.add, op1=ALU.mult)
                    ins.then_inc(sgu_out, 1)
                dve.wait_ge(mrstd_ready, l + 1)
                for t in range(NT):
                    if t < qt:
                        v = z[:, t, C_CQ:C_CKV]
                        dve.tensor_scalar(v, v, mrstd[:, t, 0:1], None, ALU.mult)
                    v = z[:, t, C_CKV:C_KR]
                    dve.tensor_scalar(v, v, mrstd[:, t, 1:2], None, ALU.mult).then_inc(mxn, 1)
                for s in range(qt // 2):
                    si = s_base[l] + s
                    dve.wait_ge(f2, si + 1)
                    wait(dve, f3, si)
                    dve.tensor_copy(fY[:, :, :], ps[:, 5, :].rearrange("p (m n) -> p m n", m=2)).then_inc(fY_ready, 1)
                for t in range(NT):
                    ai = l * NT + t
                    dve.wait_ge(qkv_mm, ai + 1)
                    wait(dve, mT2, ai - 1)
                    if t < qt:
                        src = ps[:, 5, 0:384].rearrange("p (h n) -> p h n", h=MH)
                        q_ = qm[t % 2]
                        dve.tensor_copy(q_[:, :, 0:NOPE], src[:, :, 0:NOPE])
                        if t < LT:
                            v = src[:, :, NOPE:QK].rearrange("p h (n i) -> p i h n", i=2)
                            o = q_[:, :, NOPE:QK].rearrange("p h (n i) -> p i h n", i=2)
                            link(rotate(o[:, 0, :, :], o[:, 1, :, :], v[:, 0, :, :], v[:, 1, :, :],
                                        table("cosm", t, 16, MH), table("sinm", t, 16, MH), scratch(MH, 16)))
                        else:
                            dve.tensor_copy(q_[:, :, NOPE:QK], src[:, :, NOPE:QK])
                    src = ps[:, 6, :].rearrange("p (h n) -> p h n", h=MH)
                    kr = (krr[:, t, :] if t < LT else z[:, t, C_KR:C_SG]).unsqueeze(1).broadcast_to([P, MH, ROT])
                    dve.tensor_copy(km[t % 2][:, :, 0:NOPE], src[:, :, 0:NOPE])
                    dve.tensor_copy(km[t % 2][:, :, NOPE:QK], kr)
                    dve.tensor_copy(vm[:, t, :].rearrange("p (h n) -> p h n", h=MH), src[:, :, NOPE:]).then_inc(qkv_out, 1)
                n = qt * 8
                for i in range(n + 2):
                    if i < n:
                        t, kind, hh = a_units[i]
                        g = att_base[l] + i
                        nk = NT if t < LT else NT - LT
                        c2 = slice(i % 2, i % 2 + 1)
                        dve.wait_ge(scores, g + 1)
                        wait(dve, probs_ready, g - 1)
                        if kind == 0 and t < LT:
                            o = ps[:, i % 2, (1 - t) * P:(2 - t) * P]
                            link(dve.tensor_tensor(o, o, maskv[:, t, :], ALU.add))
                        if kind == 0:
                            link(dve.tensor_reduce(nmx2[:, c2], ps[:, i % 2, 0:nk * P], AXX, ALU.max, negate=True))
                            dve.tensor_tensor(nmax[:, c2], nmx2[:, c2], nsink[:, l * WH + hh:l * WH + hh + 1],
                                              ALU.min).then_inc(smax, 1)
                        else:
                            dve.tensor_reduce(nmax[:, c2], ps[:, i % 2, 0:nk * P], AXX, ALU.max,
                                              negate=True).then_inc(smax, 1)
                    if i >= 2:
                        j = i - 2
                        t, kind, hh = a_units[j]
                        g = att_base[l] + j
                        c2 = slice(j % 2, j % 2 + 1)
                        dve.wait_ge(probs_ready, g + 1)
                        if kind == 0:
                            link(dve.tensor_tensor(rtot[:, c2], rsum[:, c2], esink[:, c2], ALU.add))
                            link(dve.reciprocal(rinv[:, c2], rtot[:, c2]))
                        else:
                            link(dve.reciprocal(rinv[:, c2], rsum[:, c2]))
                        dve.wait_ge(pv, g + 1)
                        base = (C_WQ, C_CQ)[kind] + hh * HD
                        dve.tensor_scalar(z[:, t, base:base + HD], ps[:, 4 + j % 2, 0:HD], rinv[:, c2], None,
                                          ALU.mult).then_inc(att_out, 1)

            def post(l, w):
                b0, nt, no = POST_BASE[(l, w)], POST_TILES[(l, w)], POST_NO[(l, w)]
                gate = (gate_a, gate_f)[w]
                dve.wait_ge(psq, 2 * (b0 + nt))
                link(dve.tensor_tensor(psum2[:, 0:nt], pss[:, 0:nt, 0], pss[:, 0:nt, 1], ALU.add))
                dve.tensor_scalar(pvar[:, 0:nt], psum2[:, 0:nt], 1.0 / D, EPS, ALU.mult, ALU.add).then_inc(pvar_ready, 1)
                dve.wait_ge(prstd_ready, no + 1)
                for t in range(nt):
                    for hf in range(2):
                        cs = slice(hf * 512, (hf + 1) * 512)
                        ins = dve.scalar_tensor_tensor(out=ptmp[t % 2][:, cs], in0=ps[:, hf * 4 + t, :],
                                                       scalar=prstd[:, t:t + 1], in1=gate[:, t // LT, cs],
                                                       op0=ALU.mult, op1=ALU.mult)
                    link(ins)
                    dve.tensor_tensor(h[:, t, :], h[:, t, :], ptmp[t % 2][:, :], ALU.add).then_inc(h_ready, 1)

            def out_proj(l):
                qt = QTILES[l]
                for t in range(qt):
                    b = 2 * (t % 2)
                    dve.wait_ge(mix_hi, q_base[l] + t + 1)
                    sub(actT[1][:, :, t * P:(t + 1) * P], ps[:, b:b + 2, :].rearrange("p a (c n) -> p (a c) n", c=4),
                        actT[0][:, :, t * P:(t + 1) * P]).then_inc(mix_lo, 1)
                for k in range(N_OUT):
                    split_lo(U_OUT[l] + k + 2)
                post(l, 0)

            def ffn():
                for q in range(FB // 2):
                    u = U_GU + 2 * q
                    split_lo(u + 2)
                    split_lo(u + 3)
                    dve.wait_ge(unit_used, u + 2)
                    dve.wait_ge(silu_done, q + 1)
                    b = (q % 2) * 4 + 2
                    for j in range(2):
                        ins = dve.tensor_tensor(hT[2 * q + j][:, :], ps[:, b + j, :], sgate[q % 2][:, j, :], ALU.mult)
                    ins.then_inc(hmul, 1)

                def lower(f):
                    dve.wait_ge(hth_ready, f + 1)
                    sub(htl[f % 2][:, :], hT[f][:, :], hth[f % 2][:, :]).then_inc(htl_ready, 1)

                for w in range(N_DN):
                    lower(2 * w)
                    split_lo(U_DN + w + 2)
                    lower(2 * w + 1)
                post(0, 1)

            def router():
                dve.wait_ge(wr_hi, 1)
                sub(wrl[:, :, :], wr[:, :, :], wrh[:, :, :]).then_inc(wr_ready, 1)
                dve.wait_ge(logits_mm, 1)
                link(dve.tensor_copy(logit[:, :, :], ps[:, 4, 0:LT * NE].rearrange("p (t n) -> p t n", t=LT)))
                for t in range(LT):
                    ins = dve.max(top8[:, t, :], logit[:, t, :])
                link(ins)
                for t in range(LT):
                    ins = dve.max_index(idx8[:, t, :], top8[:, t, :], logit[:, t, :])
                link(ins)
                dve.tensor_tensor(gap[:, :], top8[:, :, 1], top8[:, :, 0], ALU.subtract).then_inc(top_ready, 1)
                link(dve.tensor_copy(idxf[:, :, :], idx8[:, :, :]))
                for t in range(LT):
                    for i in range(2):
                        ins = dve.tensor_scalar(hot[:, t, i, :], K("iota8"), idxf[:, t, i:i + 1], None, ALU.is_equal)
                link(ins)
                dve.tensor_tensor(chosen[:, :, :], hot[:, :, 0, :], hot[:, :, 1, :], ALU.add).then_inc(chosen_ready, 1)
                dve.wait_ge(egap_ready, 1)
                link(dve.tensor_scalar(eden[:, :], egap[:, :], 1.0, None, ALU.add))
                link(dve.reciprocal(top_w[:, :, 0], eden[:, :]))
                link(dve.tensor_tensor(top_w[:, :, 1], egap[:, :], top_w[:, :, 0], ALU.mult))
                for t in range(LT):
                    ins = dve.tensor_scalar(cmb0[:, t, :], hot[:, t, 0, :], top_w[:, t, 0:1], None, ALU.mult)
                link(ins)
                for t in range(LT):
                    ins = dve.scalar_tensor_tensor(out=comb[:, t, :], in0=hot[:, t, 1, :], scalar=top_w[:, t, 1:2],
                                                   in1=cmb0[:, t, :], op0=ALU.mult, op1=ALU.add)
                dve.wait_ge(chosen_ready, 1)
                link(dve.tensor_scalar(away[:, :, :], chosen[:, :, :], -4096.0, 4096.0, ALU.mult, ALU.add))
                dve.wait_ge(rank_mm, 1)
                link(dve.tensor_tensor(rank[:, :, :], ps[:, 5, 0:LT * NE].rearrange("p (t n) -> p t n", t=LT),
                                       away[:, :, :], ALU.add))
                link(dve.tensor_scalar(rank1[:, :, :], rank[:, :, :], -float(P), None, ALU.add))
                link(dve.tensor_scalar(over8[:, :], ps[:, 5, LT * NE:(LT + 1) * NE], float(P), None, ALU.is_gt))
                link(dve.tensor_tensor(more_f[:, :], over8[:, :], K("left8"), ALU.mult))
                link(dve.max(more8[:, :], more_f[:, :]))
                dve.tensor_scalar(more_i[:, :], more8[:, :], 0.5, None, ALU.is_gt)
                link(dve.tensor_scalar(more_f[:, :], more8[:, :], -1.0, float(NE), ALU.mult, ALU.add))
                link(dve.memset(y[:, :, :], 0.0))
                dve.tensor_scalar(more_e[:, :], more_f[:, :], float(NE - 1), None, ALU.min).then_inc(rank_ready, 1)

            def expert(e, ee, rk):
                def esplit(k, slot_k):
                    dve.wait_ge(hi_done, ee * N_EXP + k + (U_MOE + 1))
                    sub(wlo[slot_k % NSPLIT][:, :], raw[slot_k % MRAW][:, :],
                        whi[slot_k % NSPLIT][:, :]).then_inc(lo_done, 1)

                def lower(count):
                    dve.wait_ge(e_hi, count)
                    sub(ehT[1][:, :, :], ps[:, 2, :].rearrange("p (a n) -> p a n", a=4),
                        ehT[0][:, :, :]).then_inc(e_lo, 1)

                def hidden(units, count):
                    dve.wait_ge(unit_used, units)
                    dve.wait_ge(e_silu, count)
                    dve.tensor_tensor(eh[:, :], ps[:, 1, :], esg[:, :], ALU.mult).then_inc(e_h, 1)

                for t in range(LT):
                    ins = dve.tensor_scalar(pick[:, t, :], K("iota"), rk[:, t, bass.ds(e, 1)], None, ALU.is_equal)
                ins.then_inc(pick_ready, 1)
                esplit(0, 0)
                esplit(1, 1)
                dve.wait_ge(gather_mm, ee + 1)
                modulated(gv[:, :, :].rearrange("p c n -> p (c n)"),
                          ps[:, 3:5, :].rearrange("p a (c n) -> p (a c) n", c=4), 1, 0).then_inc(gv_ready, 1)
                dve.wait_ge(pickT_mm, ee + 1)
                dve.tensor_copy(pickT[:, :, :], ps[:, 0, 0:LT * P].rearrange("p (t n) -> p t n", t=LT)).then_inc(pickT_ready, 1)
                dve.wait_ge(xg_hi_ready, ee + 1)
                sub(xg[1][:, :, :], gv[:, :, :], xg[0][:, :, :]).then_inc(xg_ready, 1)
                base = ee * N_EXP + U_MOE
                for k in range(2, 6):
                    esplit(k, k)
                hidden(base + 4, ee * EB + 1)
                with dve.Fori(1, EB) as b:
                    esplit(b * 6, 6)
                    esplit(b * 6 + 1, 7)
                    lower(ee * EB + b)
                    esplit(b * 6 + 2, 8)
                    esplit(b * 6 + 3, 9)
                    hidden(base + (b * 6 + 2), ee * EB + b + 1)
                    esplit(b * 6 + 4, 10)
                    esplit(b * 6 + 5, 11)
                lower(ee * EB + EB)
                dve.wait_ge(scat_mm, ee + 1)
                dve.wait_ge(y_added, ee)
                for t in range(LT):
                    for hf in range(2):
                        o = y[:, t, hf * 512:(hf + 1) * 512]
                        ins = dve.scalar_tensor_tensor(out=o, in0=ps[:, SCAT[2 * t + hf], :],
                                                       scalar=comb[:, t, bass.ds(e, 1)], in1=o,
                                                       op0=ALU.mult, op1=ALU.add)
                ins.then_inc(y_added, 1)

            def program():
                dve.memset(mhalf[:, :], -0.5)
                link(dve.memset(mss[:, :, :], 1.0))
                dve.wait_ge(sink_ld, 16)
                dve.tensor_scalar(nsink[:, :], sinks[:, :], -1.0, None, ALU.mult)
                dve.wait_ge(rows_T, 1)
                dve.tensor_copy(cols[:, 0:NROWS], ps[:, 0, 0:NROWS]).then_inc(cols_ready, 1)
                dve.wait_ge(silu_c, 1)
                for u in range(2):
                    split_lo(u)
                for l in range(DEPTH):
                    mod(l)
                    norm(l, 0)
                    in_proj(l)
                    mixer(l)
                    out_proj(l)
                    norm(l, 1)
                    if l == 0:
                        ffn()
                router()
                with dve.Fori(0, NE) as e:
                    expert(e, e + 0, rank)
                dve.wait_ge(rank_ready, 1)
                with dve.Fori(0, MAX_OVER) as i:
                    more = dve.value_load(more_i[0:1, bass.ds(i, 1)], min_val=0, max_val=1)
                    with dve.If(more):
                        e = dve.value_load(more_e[0:1, bass.ds(i, 1)], min_val=0, max_val=NE - 1)
                        expert(e, i + NE, rank1)
                    dve.engine_nop()
                dve.engine_nop().then_inc(y_done, 1)
                dve.wait_ge(fsq, LT)
                dve.tensor_scalar(pvar[:, 0:LT], pss[:, 0:LT, 0], 1.0 / D, EPS, ALU.mult, ALU.add).then_inc(fvar, 1)
                dve.wait_ge(frstd, 1)
                for t in range(LT):
                    link(dve.scalar_tensor_tensor(out=y[:, t, :], in0=y[:, t, :], scalar=prstd[:, t:t + 1],
                                                  in1=gate_f[:, 0, :], op0=ALU.mult, op1=ALU.mult))
                    dve.tensor_tensor(h[:, t, :], h[:, t, :], y[:, t, :], ALU.add).then_inc(fin, 1)

            program()


def gate_no(l, b):
    g = [(ll, bb) for ll in range(DEPTH) for bb in range(MOD_BLOCKS) if bb // 2 in (2, 5)]
    return g.index((l, b))


SCAT = [7, 3, 4, 2]


def shape_constants():
    t = {}
    i = np.arange(P)
    t["ident"] = np.eye(P)
    n = np.arange(SEQ)
    ang = 2 * np.pi * (np.outer(n, n) % SEQ) / SEQ
    cs = np.concatenate([np.cos(ang), np.sin(ang)], axis=1).reshape(2, P, 2 * SEQ)
    t["dft"] = cs.transpose(1, 0, 2).reshape(P, -1)
    ch = GW // 4
    m = np.arange(ch)
    ang = 2 * np.pi * (np.outer(m, m) % ch) / ch
    scale = (SEQ * ch) ** -0.5
    t["cch"] = np.kron(np.eye(2), np.cos(ang)) * scale
    t["nsch"] = -np.kron(np.eye(2), np.sin(ang)) * scale
    q, k = np.meshgrid(i, i, indexing="ij")
    masks = []
    for tile in range(2):
        far = np.abs((k + (1 - tile) * P) - (q + tile * P)) > WINDOW
        masks.append(np.where(far, -1e30, 0.0))
    t["mask"] = np.concatenate(masks, axis=1)
    for suffix, dim in (("w", HD), ("m", ROT)):
        nf = dim // 4
        inv = (np.float32(10000.0) ** (-np.arange(nf, dtype=np.float32) / nf)).astype(np.float32)
        row = np.repeat(np.arange(SEQ // GRID_W, dtype=np.float32), GRID_W)
        col = np.tile(np.arange(GRID_W, dtype=np.float32), SEQ // GRID_W)
        a = np.concatenate([row[:, None] * inv, col[:, None] * inv], axis=-1).astype(np.float64)
        for fn, nm in ((np.cos, "cos"), (np.sin, "sin")):
            t[nm + suffix] = fn(a).reshape(2, P, -1).transpose(1, 0, 2).reshape(P, -1)
    t["iota"] = np.tile(i[None, :], (P, 1))
    t["before"] = (i[:, None] < i[None, :]).astype(float)
    t["ones"] = np.ones((P, P))
    sr = np.zeros((P, 2, P))
    sc = np.zeros((P, 2))
    for s in range(2):
        sr[[s, 2 + s, 4], s, :] = 1.0
        sc[[s, 2 + s, 4], s] = 1.0
    t["selrow"] = sr.reshape(P, -1)
    t["selcol"] = sc
    t["iota8"] = np.tile(np.arange(NE)[None, :], (P, 1))
    t["left8"] = NE - t["iota8"]
    return np.concatenate([t[name] for name, _ in CONST_COLS], axis=1).astype(np.float32)


_INS = ['x', 'c', 'ctx', 'c_ctx', 'w_mod', 'b_mod', 'g_pre_mix', 'g_post_mix', 'g_pre_ffn', 'g_post_ffn', 'w_in', 'w_out',
        'w_fourier', 'win_sink', 'mla_g_q', 'mla_g_kv', 'mla_w_uq', 'mla_w_ukv', 'sgu_w', 'sgu_b', 'ffn_w_gate',
        'ffn_w_up', 'ffn_w_down', 'moe_w_router', 'moe_w_gate', 'moe_w_up', 'moe_w_down']


def kernel(**inputs):
    import concourse.bacc as bacc
    from concourse.bass_utils import run_bass_kernel_spmd

    nc = bacc.Bacc("TRN2", target_bir_lowering=False, num_devices=1)
    arrays = {f"in_{name}": np.ascontiguousarray(inputs[name]) for name in _INS}
    arrays["in_consts"] = shape_constants()
    args = [nc.dram_tensor(n, a.shape, mybir.dt.from_np(a.dtype), kind="ExternalInput").ap() for n, a in arrays.items()]
    out = nc.dram_tensor("out", (1, SEQ, D), F32, kind="ExternalOutput").ap()
    build(nc, *args, out)
    r = run_bass_kernel_spmd(nc, [arrays], core_ids=[0])
    return r.results[0]["out"]
```

```python
from contextlib import ExitStack

import numpy as np

import concourse.bass as bass
from concourse import mybir

ALU = mybir.AluOpType
ACT = mybir.ActivationFunctionType
AXX = mybir.AxisListType.X
F32 = mybir.dt.float32
F32R = mybir.dt.float32r
I32 = mybir.dt.int32
U32 = mybir.dt.uint32

P = 128
D = 1024
SEQ = 256
CTX = 256
DEPTH = 2
GRID_W = 64
NT = (SEQ + CTX) // P
LT = SEQ // P
KC = D // P
GW = D // 4
HD = 64
WH, KVH = 4, 2
MH, NOPE, ROT, QK = 4, 64, 32, 96
D_FF = 3584
FB = D_FF // P
NE = 8
WINDOW = 128
EPS = 1e-6
DIN = 1696
C_A, C_WQ, C_WK, C_WV, C_CQ, C_CKV, C_KR, C_SG = 0, 256, 512, 640, 768, 1024, 1152, 1184
MIX_COLS = [C_A, C_A + P, C_WQ, C_WQ + P, C_CQ, C_CQ + P, C_SG, C_SG + P]

R_C, R_CTX, R_PRE_MIX, R_PRE_FFN, R_GQ, R_GKV, R_SGB, NROWS = 0, 8, 16, 32, 48, 52, 54, 62

CONST_COLS = [("ident", P), ("dft", 2 * 512), ("cch", P), ("nsch", P), ("mask", 2 * P), ("cosw", 64), ("sinw", 64),
              ("cosm", 32), ("sinm", 32), ("iota", P), ("before", P), ("ones", P), ("selcol", 2),
              ("iota8", 8), ("left8", 8)]
CONST_AT = {}
_at = 0
for _name, _n in CONST_COLS:
    CONST_AT[_name] = (_at, _at + _n)
    _at += _n
NCONST = _at

UNIT = 2048
MOD_BLOCKS = 6 * D // 512
IN_BLOCKS, IN_W = 4, DIN // 4
N_MOD, N_IN, N_OUT = 2 * MOD_BLOCKS, 2 * IN_BLOCKS, 4
N_GU, N_DN = FB, FB // 2
U_GU = N_MOD + N_IN + N_OUT
U_DN = U_GU + N_GU + N_MOD
U_IN = [N_MOD, U_DN + N_DN]
U_OUT = [u + N_IN for u in U_IN]
U_MOE = U_OUT[1] + N_OUT
NRAW, NSPLIT = 3, 3
MRAW = 6
EB = D_FF // 512
N_EXP = 6 * EB
MAX_OVER = 2 * SEQ // (P + 1)
NR = NE + MAX_OVER + 1
assert U_MOE % NSPLIT == 0 and N_EXP % MRAW == 0


def gu_unit(q):
    return U_GU + 2 * q + 2 * min(q, MOD_BLOCKS)


def mod_unit(l, b):
    return 2 * b if l == 0 else gu_unit(b) + 2


QTILES = [NT, LT]
NORM_BASE = {(0, 0): 0, (0, 1): 4, (1, 0): 8, (1, 1): 12}
NORM_TILES = {(0, 0): 4, (0, 1): 4, (1, 0): 4, (1, 1): 2}
POST_BASE = {(0, 0): 0, (0, 1): 4, (1, 0): 8}
NEXT = {(0, 0): (0, 1), (0, 1): (1, 0), (1, 0): (1, 1)}
BRANCH_BASE = {(0, 0): 0, (0, 1): 3, (1, 0): 6}
POST_TILES = {(0, 0): 4, (0, 1): 4, (1, 0): 2}
KB = 1024


def build(nc, x, c, ctx_in, c_ctx, w_mod, b_mod, g_pre_mix, g_post_mix, g_pre_ffn, g_post_ffn, w_in, w_out,
          w_fourier, win_sink, mla_g_q, mla_g_kv, mla_w_uq, mla_w_ukv, sgu_w, sgu_b, ffn_w_gate, ffn_w_up,
          ffn_w_down, moe_w_router, moe_w_gate, moe_w_up, moe_w_down, consts, out):
    with ExitStack() as stack:
        def sem(name):
            return stack.enter_context(nc.semaphore(name))

        def at(name, shape, kb, dt=F32):
            return nc.alloc_sbuf_tensor_at(name, shape, dt, offset=BASE + int(kb * KB))

        BASE = -(-nc.sbuf_base // 32) * 32
        raw = [at(f"raw{i}", [P, UNIT], 8 * i) for i in range(MRAW)]
        whi = [at(f"whi{i}", [P, UNIT], 48 + 8 * i, F32R) for i in range(NSPLIT)]
        wlo = [at(f"wlo{i}", [P, UNIT], 72 + 8 * i, F32R) for i in range(NSPLIT)]
        h = at("h", [P, NT, D], 96)
        const_base = 112
        con = at("con", [P, NCONST], const_base)
        top = [-(-(const_base * KB + 4 * NCONST) // 32) * 32]

        def small(name, shape, dt=F32):
            n = int(np.prod(shape[1:])) * 4
            t = nc.alloc_sbuf_tensor_at(name, shape, dt, offset=BASE + top[0])
            top[0] += -(-n // 32) * 32
            return t

        cols = small("cols", [P, NROWS + 2])
        condf = small("condf", [P, 2 * KC])
        acol = small("acol", [P, 2, 2, KC])
        bcol = small("bcol", [P, 2, 2, KC])
        sinks = small("sinks", [P, DEPTH * WH])
        nsink = small("nsink", [P, DEPTH * WH])
        mhalf = small("mhalf", [P, 8])
        ss = small("ss", [P, 4])
        var = small("var", [P, 4])
        rstd = small("rstd", [P, 4])
        pss = small("pss", [P, 4])
        pvar = small("pvar", [P, 4])
        prstd = small("prstd", [P, 4])
        bst = small("bst", [P, 4, 6])
        mv = small("mv", [P, 4, 2])
        svar = small("svar", [P, 4])
        srstd = small("srstd", [P, 4])
        mss = small("mss", [P, 4, 2])
        mvar = small("mvar", [P, 4, 2])
        mrstd = small("mrstd", [P, 4, 2])
        krr = small("krr", [P, 2, ROT])
        nmax = small("nmax", [P, 4])
        nmx2 = small("nmx2", [P, 4])
        rsum = small("rsum", [P, 4])
        esink = small("esink", [P, 4])
        rtot = small("rtot", [P, 4])
        rinv = small("rinv", [P, 4])
        wr = small("wr", [P, KC, NE])
        wrh = small("wrh", [P, KC, NE], F32R)
        wrl = small("wrl", [P, KC, NE], F32R)
        logit = small("logit", [P, LT, NE])
        top8 = small("top8", [P, LT, NE])
        idx8 = small("idx8", [P, LT, NE], U32)
        idxf = small("idxf", [P, LT, NE])
        gap = small("gap", [P, LT])
        egap = small("egap", [P, LT])
        eden = small("eden", [P, LT])
        top_w = small("top_w", [P, LT, 2])
        hot = small("hot", [P, LT, 2, NE])
        slot_of = small("slot_of", [P, LT, NR])
        weight_of = small("weight_of", [P, LT, NR])
        round_e = small("round_e", [P, NR], I32)
        late = small("late", [P, MAX_OVER, NE])
        late_r = small("late_r", [P, LT, MAX_OVER, NE])
        late_w = small("late_w", [P, LT, MAX_OVER, NE])
        gcol = small("gcol", [P, 2, 2, KC])
        cmb0 = small("cmb0", [P, LT, NE])
        chosen = small("chosen", [P, LT, NE])
        away = small("away", [P, LT, NE])
        rank1 = small("rank1", [P, LT, NE])
        over8 = small("over8", [P, NE])
        more8 = small("more8", [P, NE])
        more_f = small("more_f", [P, NE])
        more_i = small("more_i", [P, NE], I32)
        G0 = 125.25
        assert top[0] <= G0 * KB, top[0]
        gate_f = at("gate_f", [P, 2, D], G0)
        gate_a = at("gate_a", [P, 2, D], G0 + 8)
        Z0 = G0 + 16
        z = at("z", [P, NT, DIN], Z0)
        S0 = Z0 + 26.5
        actT = [at("actT_hi", [P, KC, NT * P], S0, F32R), at("actT_lo", [P, KC, NT * P], S0 + 16, F32R)]
        junk = at("junk", [P, D], Z0)
        xh = [at(f"xh{i}", [P, D], Z0 + 4 + 4 * i) for i in range(2)]
        modv = [at(f"modv{i}", [P, D], Z0 + 12 + 4 * i) for i in range(2)]
        ptmp = at("ptmp", [P, D], Z0 + 20)
        bjunk = [at("bjunk0", [P, D], S0 + 32), at("bjunk1", [P, D], 24)]
        X0 = 24
        w_uq = at("w_uq", [P, 2, MH * QK], X0)
        w_ukv = at("w_ukv", [P, MH * (NOPE + HD)], X0 + 3)
        w_four = at("w_four", [P, 2, GW], X0 + 5)
        sgw = at("sgw", [P, 4, P], X0 + 7)
        sgwT = at("sgwT", [P, 4, P], X0 + 9)
        mrow = [at(f"mrow{i}", [P, 512], (X0 + 22, X0 + 11)[i]) for i in range(2)]
        rope_s = [at(f"rope_s{i}", [P, 192], X0 + 15 + 0.75 * i) for i in range(4)]
        rows = at("rows", [64, P], X0 + 18)
        mjunk = at("mjunk", [P, 256], X0 + 19)
        cond4 = at("cond4", [P, KC, P], S0 + 36, F32R)
        qTw = at("qTw", [P, 2, NT * P], S0)
        kTw = at("kTw", [P, NT * P], S0 + 4)
        qTm = at("qTm", [P, MH, NT * P], S0 + 6)
        kTm = at("kTm", [P, MH, NT * P], S0 + 14)
        fU = at("fU", [P, 2, 512], S0 + 6)
        fY = at("fY", [P, 2, 256], S0 + 10)
        vm = at("vm", [P, NT, GW], S0 + 22)
        qkr = at("qkr", [P, LT, 384], S0 + 26)
        qctx = at("qctx", [P, LT, 256], X0 + 21.5)
        cqT = at("cqT", [P, 2, NT * P], S0 + 29)
        ckvT = at("ckvT", [P, NT * P], S0 + 33)
        qm = [at(f"qm{i}", [P, MH, QK], S0 + 35 + 1.5 * i) for i in range(2)]
        km = [at(f"km{i}", [P, MH, QK], (S0 + 38, X0 + 20)[i]) for i in range(2)]
        probs = [at(f"probs{i}", [P, 512], S0 + 26 + 2 * i) for i in range(2)]
        probT = [at(f"probT{i}", [P, 512], S0 + 30 + 2 * i) for i in range(2)]
        hT = [at(f"hT{f}", [P, NT * P], G0 + 8 + 2 * f if f < 17 else X0 + 2 * (f - 17)) for f in range(FB)]
        sgate = at("sgate", [P, 2, 512], S0 + 32)
        hth = [at(f"hth{i}", [P, NT * P], S0 + 32 + 2 * i, F32R) for i in range(2)]
        htl = [at(f"htl{i}", [P, NT * P], S0 + 36 + 2 * i, F32R) for i in range(2)]
        y = at("y", [P, LT, D], S0 + 32)
        xg = [at("xg_hi", [P, KC, P], S0, F32R), at("xg_lo", [P, KC, P], S0 + 4, F32R)]
        gv = at("gv", [P, KC, P], S0 + 8)
        eh = at("eh", [P, 512], S0 + 12)
        esg = at("esg", [P, 512], S0 + 14)
        ehT = [at("ehT_hi", [P, 4, P], S0 + 16, F32R), at("ehT_lo", [P, 4, P], S0 + 18, F32R)]
        pick = at("pick", [P, LT, P], S0 + 20)
        pickT = at("pickT", [P, LT, P], S0 + 21)
        ysb = at("ysb", [P, D], S0 + 22)

        ps = stack.enter_context(nc.psum_tensor("ps", [P, 8, 512], F32))

        def K(name):
            a, b = CONST_AT[name]
            return con[:, a:b]

        ident = K("ident")
        dft = K("dft").rearrange("p (k n) -> p k n", k=2)
        maskv = K("mask").rearrange("p (t n) -> p t n", t=2)

        def rot(name, t, n):
            return K(name).rearrange("p (t n) -> p t n", t=2)[:, t, 0:n]

        con_ld, cond_ld, rows_ld, h_ld, sink_ld, wr_ld = (sem(n) for n in ("con_ld", "cond_ld", "rows_ld", "h_ld", "sink_ld", "wr_ld"))
        raw_full = [sem(f"raw_full{i}") for i in range(MRAW)]
        hi_done, lo_done, unit_used = sem("hi_done"), sem("lo_done"), sem("unit_used")
        rows_T, cols_ready, silu_c, cond_ready = sem("rows_T"), sem("cols_ready"), sem("silu_c"), sem("cond_ready")
        bmod_ld = [sem("bmod_ld0"), sem("bmod_ld1")]
        gpost_ld, small_ld, mrow_ready, mod_used = sem("gpost_ld"), sem("small_ld"), sem("mrow_ready"), sem("mod_used")
        gate_mm, gate_done, modc_ready = sem("gate_mm"), sem("gate_done"), sem("modc_ready")
        sq_done, var_ready, rstd_ready, xh_ready = sem("sq_done"), sem("var_ready"), sem("rstd_ready"), sem("xh_ready")
        xhT_ready, modv_ready, acthi, actlo = sem("xhT_ready"), sem("modv_ready"), sem("acthi"), sem("actlo")
        z_act, z_dve = sem("z_act"), sem("z_dve")
        gelu_done, svar_ready, srstd_ready, sv_ready = sem("gelu_done"), sem("svar_ready"), sem("srstd_ready"), sem("sv_ready")
        sgw_T, sgw_ready, sgu_mm, sgu_out = sem("sgw_T"), sem("sgw_ready"), sem("sgu_mm"), sem("sgu_out")
        f1, fU_ready, f2, fY_ready, f3, four_out = (sem(n) for n in ("f1", "fU_ready", "f2", "fY_ready", "f3", "four_out"))
        rope_done, qctx_ready, winT, winT_out = sem("rope_done"), sem("qctx_ready"), sem("winT"), sem("winT_out")
        msq, mvar_ready, mrstd_ready, mxn = sem("msq"), sem("mvar_ready"), sem("mrstd_ready"), sem("mxn")
        mT, mT_out, qkv_mm, qkv_out, mT2, mT2_out = (sem(n) for n in ("mT", "mT_out", "qkv_mm", "qkv_out", "mT2", "mT2_out"))
        scores, smax, probs_ready, probs_T, probT_ready, pv, att_out = (
            sem(n) for n in ("scores", "smax", "probs_ready", "probs_T", "probT_ready", "pv", "att_out"))
        mixT, mix_hi, mix_lo, branch_done = sem("mixT"), sem("mix_hi"), sem("mix_lo"), sem("branch_done")
        psq, pvar_ready, prstd_ready, h_ready = sem("psq"), sem("pvar_ready"), sem("prstd_ready"), sem("h_ready")
        silu_done, hmul, hth_ready, htl_ready, even_used = (
            sem(n) for n in ("silu_done", "hmul", "hth_ready", "htl_ready", "even_used"))
        wr_hi, wr_ready, logits_mm, top_ready, egap_ready, chosen_ready, rank_mm, rank_ready = (
            sem(n) for n in ("wr_hi", "wr_ready", "logits_mm", "top_ready", "egap_ready", "chosen_ready", "rank_mm", "rank_ready"))
        pick_ready, gather_mm, pickT_mm, pickT_ready, gv_ready, xg_hi_ready, xg_ready = (
            sem(n) for n in ("pick_ready", "gather_mm", "pickT_mm", "pickT_ready", "gv_ready", "xg_hi_ready", "xg_ready"))
        e_silu, e_h, e_T, e_hi, e_lo, e_down, ysb_ready, scat_mm, y_added = (
            sem(n) for n in ("e_silu", "e_h", "e_T", "e_hi", "e_lo", "e_down", "ysb_ready", "scat_mm", "y_added"))
        y_done, fsq, fvar, frstd, fin, stored = (sem(n) for n in ("y_done", "fsq", "fvar", "frstd", "fin", "stored"))
        dve_c, act_c = sem("dve_c"), sem("act_c")
        chain = {"dve": 0, "act": 0}

        def wait(e, s, n):
            if isinstance(n, int) and n <= 0:
                return
            e.wait_ge(s, n)

        raw_before = [U_MOE // NRAW] * NRAW + [0] * (MRAW - NRAW)

        def in_tiles(l, b):
            return NT if l == 0 or b in (1, 2) else LT

        def mbuf(l, b):
            return b % 2 if l == 0 else 0

        def mbias(l, b):
            return b // 2 + 1 if l == 0 else MOD_BLOCKS // 2 + b + 1

        def zdve_count(l, b):
            return sum(1 for ll in range(DEPTH) for bb in range(IN_BLOCKS)
                       if (ll, bb) <= (l, b) and in_tiles(ll, bb) == NT)

        q_base = [0, QTILES[0]]
        s_base = [0, QTILES[0] // 2]
        a_units = [(t, kind, hh) for t in range(NT) for kind in (0, 1) for hh in range(4)]
        gate_base = [0, QTILES[0]]
        att_base = [0, QTILES[0] * 8]

        block = stack.enter_context(nc.Block())


        @block.sync
        def _(sp):
            def load(u, src):
                s = u % NRAW
                wait(sp, lo_done, u - NRAW + 1)
                dst = raw[s][:, 0:int(np.prod(src.shape[1:]))].rearrange("p (a b) -> p a b", a=src.shape[1])
                sp.dma_start(dst, src).then_inc(raw_full[s], 16)

            def halves(w, ncols, b, half):
                return w.rearrange("(c p) n -> p c n", p=P)[:, 4 * half:4 * half + 4, b * ncols:(b + 1) * ncols]

            def program():
                sp.dma_start(rows[R_C:R_C + 8, :], c.rearrange("a (r n) -> (a r) n", n=P)).then_inc(cond_ld, 16)
                sp.dma_start(rows[R_CTX:R_CTX + 8, :], c_ctx.rearrange("(r n) -> r n", n=P)).then_inc(cond_ld, 16)
                sp.dma_start(con[:, :], consts).then_inc(con_ld, 16)
                for l in range(DEPTH):
                    for b in range(MOD_BLOCKS if l == 0 else 0):
                        for half in range(2):
                            load(mod_unit(0, b) + half, halves(w_mod[0], 512, b, half))
                    for b in range(IN_BLOCKS):
                        for half in range(2):
                            load(U_IN[l] + 2 * b + half, halves(w_in[l], IN_W, b, half))
                    for b in range(2):
                        for half in range(2):
                            load(U_OUT[l] + 2 * b + half, halves(w_out[l], 512, b, half))
                    if l == 0:
                        gate_v, up_v = (w[0].rearrange("(c p) n -> p c n", p=P) for w in (ffn_w_gate, ffn_w_up))
                        down_v = ffn_w_down[0].rearrange("(f p) n -> p f n", p=P)
                        for q in range(FB // 2):
                            load(gu_unit(q), gate_v[:, :, q * 256:(q + 1) * 256])
                            load(gu_unit(q) + 1, up_v[:, :, q * 256:(q + 1) * 256])
                            for half in range(2 if q < MOD_BLOCKS else 0):
                                load(mod_unit(1, q) + half, halves(w_mod[1], 512, q, half))
                        for w in range(N_DN):
                            load(U_DN + w, down_v[:, 2 * w:2 * w + 2, :])
                gv_ = moe_w_gate[0].rearrange("e (a c p) n -> e a p c n", p=P, c=4)
                uv_ = moe_w_up[0].rearrange("e (a c p) n -> e a p c n", p=P, c=4)
                dv_ = moe_w_down[0].rearrange("e (f p) n -> e p f n", p=P)

                def eload(k, ee, slot_k, src):
                    sp.wait_ge(lo_done, ee * N_EXP + k + (U_MOE - MRAW + 1))
                    sp.dma_start(raw[slot_k % MRAW][:, :].rearrange("p (a b) -> p a b", a=src.shape[1]),
                                 src).then_inc(raw_full[slot_k % MRAW], 16)

                def expert(e, ee):
                    for half in range(2):
                        eload(2 + half, ee, 2 + half, uv_[e, half, :, :, 0:512])
                    with sp.Fori(1, EB) as b:
                        cols_b = bass.ds(b * 512, 512)
                        for half in range(2):
                            eload(b * 6 + (half - 2), ee, 4 + half, gv_[e, half, :, :, cols_b])
                        for half in range(2):
                            eload(b * 6 + half, ee, 6 + half, uv_[e, half, :, :, cols_b])
                        for half in range(2):
                            eload(b * 6 + (2 + half), ee, 8 + half, dv_[e, :, bass.ds(b * 4 + (2 * half - 4), 2), :])
                    for half in range(2):
                        eload(40 + half, ee, 40 + half, dv_[e, :, 4 * EB - 4 + 2 * half:4 * EB - 2 + 2 * half, :])
                    sp.wait_ge(rank_ready, 1)
                    following = sp.value_load(round_e[0:1, bass.ds(ee + 1, 1)], min_val=0, max_val=NE - 1)
                    for half in range(2):
                        eload(N_EXP + half, ee, half, gv_[following, half, :, :, 0:512])

                for half in range(2):
                    sp.wait_ge(lo_done, U_MOE - NRAW + half + 1)
                    sp.dma_start(raw[half][:, :].rearrange("p (a b) -> p a b", a=4),
                                 gv_[0, half, :, :, 0:512]).then_inc(raw_full[half], 16)
                sp.wait_ge(lo_done, U_MOE)
                sp.wait_ge(att_out, att_base[1] + 8 * LT)
                with sp.Fori(0, NE) as e:
                    expert(e, e + 0)
                with sp.Fori(0, MAX_OVER) as i:
                    more = sp.value_load(more_i[0:1, bass.ds(i, 1)], min_val=0, max_val=1)
                    with sp.If(more):
                        e = sp.value_load(round_e[0:1, bass.ds(i + NE, 1)], min_val=0, max_val=NE - 1)
                        expert(e, i + NE)
                    sp.nop()
                sp.wait_ge(fin, LT)
                for t in range(LT):
                    sp.dma_start(out[0, t * P:(t + 1) * P, :], h[:, t, :]).then_inc(stored, 16)
                sp.wait_ge(stored, 16 * LT)

            program()

        @block.gpsimd
        def _(pool):
            def power(dst, src, n, ready, count, done):
                pool.wait_ge(ready, count)
                pool.tensor_tensor(dst, src, mhalf[:, 0:n], ALU.pow).then_inc(done, 1)

            def layer_loads(l):
                if l:
                    pool.wait_ge(h_ready, POST_BASE[(0, 1)] + NT)
                for i in range(QTILES[l] // LT):
                    pool.dma_start(gate_a[:, i, :], g_post_mix[l].partition_broadcast(P)).then_inc(gpost_ld, 16)
                    pool.dma_start(gate_f[:, i, :], g_post_ffn[l].partition_broadcast(P)).then_inc(gpost_ld, 16)
                pool.dma_start(w_uq[:, :, :], mla_w_uq[l].rearrange("(c p) n -> p c n", p=P)).then_inc(small_ld, 16)
                pool.dma_start(w_ukv[:, :], mla_w_ukv[l]).then_inc(small_ld, 16)
                pool.dma_start(w_four[:, :, :], w_fourier[l].rearrange("(c p) n -> p c n", p=P)).then_inc(small_ld, 16)
                pool.dma_start(sgw[:, :, :], sgu_w[l].rearrange("g p q -> p g q")).then_inc(small_ld, 16)

            def norm_power(n0, t):
                power(rstd[:, t:t + 1], var[:, t:t + 1], 1, var_ready, n0 + t + 1, rstd_ready)

            def finish_power(l, w):
                b0, n0 = POST_BASE[(l, w)], NORM_BASE[NEXT[(l, w)]]
                for t in range(POST_TILES[(l, w)] + 1):
                    if t < POST_TILES[(l, w)]:
                        power(prstd[:, t:t + 1], pvar[:, t:t + 1], 1, pvar_ready, b0 + t + 1, prstd_ready)
                    if t:
                        norm_power(n0, t - 1)

            def bias_rows(l):
                for b in range(MOD_BLOCKS):
                    gb = l * MOD_BLOCKS + b
                    wait(pool, mod_used, gb - 1 + l)
                    pool.dma_start(mrow[mbuf(l, b)][4:5, :], b_mod[l:l + 1, b * 512:(b + 1) * 512]).then_inc(
                        bmod_ld[mbuf(l, b)], 16)

            def program():
                for r, src in ((R_PRE_MIX, g_pre_mix), (R_PRE_FFN, g_pre_ffn), (R_GQ, mla_g_q), (R_GKV, mla_g_kv)):
                    v = src.rearrange("l (r n) -> (l r) n", n=P)
                    pool.dma_start(rows[r:r + v.shape[0], :], v).then_inc(rows_ld, 16)
                pool.dma_start(rows[R_SGB:R_SGB + 8, :], sgu_b.rearrange("l g n -> (l g) n")).then_inc(rows_ld, 16)
                for t in range(NT):
                    src = x if t < LT else ctx_in
                    pool.dma_start(h[:, t, :], src[0, (t % LT) * P:(t % LT + 1) * P, :]).then_inc(h_ld, 16)
                pool.dma_start(sinks[:, :], win_sink.rearrange("l h -> (l h)").partition_broadcast(P)).then_inc(sink_ld, 16)
                pool.dma_start(wr[:, :, :], moe_w_router[0].rearrange("(c p) n -> p c n", p=P)).then_inc(wr_ld, 16)
                for l in range(DEPTH):
                    layer_loads(l)
                    if l == 0:
                        bias_rows(0)
                    for t in range(NT if l == 0 else 0):
                        norm_power(0, t)
                    q = QTILES[l]
                    power(srstd[:, 0:q], svar[:, 0:q], q, svar_ready, l + 1, srstd_ready)
                    power(mrstd[:, :, :].rearrange("p a b -> p (a b)"), mvar[:, :, :].rearrange("p a b -> p (a b)"), 8,
                          mvar_ready, l + 1, mrstd_ready)
                    finish_power(l, 0)
                    if l == 0:
                        bias_rows(1)
                        finish_power(0, 1)
                power(prstd[:, 0:2], pvar[:, 0:2], 2, fvar, 1, frstd)

            program()

        @block.scalar
        def _(act):
            def copy(dst, src, **kw):
                return act.activation(dst, src, ACT.Copy, **kw)

            def split_hi(u):
                if u >= U_MOE:
                    return
                act.wait_ge(raw_full[u % NRAW], 16 * (u // NRAW + 1))
                wait(act, unit_used, u - NSPLIT + 1)
                n = 4 * IN_W if U_IN[0] <= u < U_OUT[0] or U_IN[1] <= u < U_OUT[1] else UNIT
                copy(whi[u % NSPLIT][:, 0:n], raw[u % NRAW][:, 0:n]).then_inc(hi_done, 1)

            def first_norm():
                act.wait_ge(h_ld, 16 * NT)
                for t in range(NT):
                    square_h(0, t)
                act.wait_ge(modc_ready, 1)
                for t in range(NT):
                    modulate(0, 0, t)

            def in_proj(l):
                for b in range(IN_BLOCKS):
                    for half in range(2):
                        split_hi(U_IN[l] + 2 * b + half + 2)
                    act.wait_ge(unit_used, U_IN[l] + 2 * b + 2)
                    for t in range(LT):
                        ins = copy(z[:, t, b * IN_W:(b + 1) * IN_W], ps[:, (b % 2) * 4 + t, 0:IN_W])
                    ins.then_inc(z_act, 1)

            def mixer(l):
                qt = QTILES[l]
                act.wait_ge(z_dve, zdve_count(l, IN_BLOCKS - 1))
                act.wait_ge(z_act, IN_BLOCKS * (l + 1))
                for t in range(qt):
                    act.activation(z[:, t, C_SG:DIN], z[:, t, C_SG:DIN], ACT.Gelu).then_inc(gelu_done, 1)
                done = l * 2 * NT
                for t in range(NT):
                    if t < qt:
                        wait(act, msq, done)
                        act.activation(mjunk[:, :], z[:, t, C_CQ:C_CKV], ACT.Square,
                                       accum_out=mss[:, t, 0:1]).then_inc(msq, 1)
                        done += 1
                    wait(act, msq, done)
                    done += 1
                    act.activation(mjunk[:, 0:P], z[:, t, C_CKV:C_KR], ACT.Square,
                                   accum_out=mss[:, t, 1:2]).then_inc(msq, 1)
                for s in range(qt // 2):
                    si = s_base[l] + s
                    act.wait_ge(f1, si + 1)
                    wait(act, f2, si)
                    copy(fU[:, :, :], ps[:, 3:5, :]).then_inc(fU_ready, 1)
                    act.wait_ge(f3, si + 1)
                    copy(z[:, 2 * s:2 * s + 2, 0:GW], ps[:, 6, :].rearrange("p (k n) -> p k n", k=2)).then_inc(four_out, 1)
                for t in range(NT):
                    b = 1 + t % 2
                    act.wait_ge(winT, l * NT + t + 1)
                    if t < qt:
                        copy(qTw[:, :, t * P:(t + 1) * P], ps[:, b, 0:256].rearrange("p (a n) -> p a n", a=2),
                             scale=HD ** -0.5)
                    copy(kTw[:, t * P:(t + 1) * P], ps[:, b, 256:384]).then_inc(winT_out, 1)
                for i in range(NT + 2):
                    if i < NT:
                        t = i
                        b = 3 + t % 2
                        act.wait_ge(mT, l * NT + t + 1)
                        if t < qt:
                            for j in range(2):
                                copy(cqT[:, j, t * P:(t + 1) * P], ps[:, b, j * P:(j + 1) * P],
                                     scale=cols[:, R_GQ + 2 * l + j:R_GQ + 2 * l + j + 1])
                        copy(ckvT[:, t * P:(t + 1) * P], ps[:, b, 256:384],
                             scale=cols[:, R_GKV + l:R_GKV + l + 1]).then_inc(mT_out, 1)
                    if i >= 2:
                        t = i - 2
                        act.wait_ge(mT2, l * NT + t + 1)
                        if t < qt:
                            copy(qTm[0:QK, :, t * P:(t + 1) * P], ps[0:QK, 7, :].rearrange("p (a n) -> p a n", a=4),
                                 scale=QK ** -0.5)
                        copy(kTm[0:QK, :, t * P:(t + 1) * P],
                             ps[0:QK, 0, :].rearrange("p (a n) -> p a n", a=4)).then_inc(mT2_out, 1)
                n = qt * 8
                for i in range(n + 2):
                    if i < n:
                        t, kind, hh = a_units[i]
                        g = att_base[l] + i
                        nk = NT if t < LT else NT - LT
                        c4 = slice(i % 4, i % 4 + 1)
                        act.wait_ge(smax, g + 1)
                        wait(act, probs_T, g - 1)
                        wait(act, att_out, g - 3)
                        if kind == 0:
                            act.activation(esink[:, c4], sinks[:, l * WH + hh:l * WH + hh + 1], ACT.Exp,
                                           bias=nmax[:, c4])
                        act.activation(probs[i % 2][:, 0:nk * P], ps[:, SCORE[i % 4], 0:nk * P], ACT.Exp,
                                       bias=nmax[:, c4], accum_out=rsum[:, c4]).then_inc(probs_ready, 1)
                    if i >= 2:
                        j = i - 2
                        g = att_base[l] + j
                        nk = NT if a_units[j][0] < LT else NT - LT
                        act.wait_ge(probs_T, g + 1)
                        wait(act, pv, g - 1)
                        copy(probT[j % 2][:, 0:nk * P], ps[:, 2 + j % 2, 0:nk * P]).then_inc(probT_ready, 1)

            def square_h(n0, t):
                if n0 + t:
                    act.wait_ge(sq_done, n0 + t)
                act.activation(junk[:, :], h[:, t, :], ACT.Square, accum_out=ss[:, t:t + 1]).then_inc(sq_done, 1)

            def modulate(l, w, t):
                n0 = NORM_BASE[(l, w)]
                act.wait_ge(xhT_ready, n0 + t + 1)
                wait(act, actlo, n0 + t - 1)
                for k in range(KC):
                    ins = act.activation(modv[t % 2][:, k * P:(k + 1) * P],
                                         ps[:, 2 * t + k // 4, (k % 4) * P:(k % 4 + 1) * P], ACT.Identity,
                                         scale=acol[:, w, t // LT, k:k + 1], bias=bcol[:, w, t // LT, k:k + 1])
                ins.then_inc(modv_ready, 1)
                act.wait_ge(modv_ready, n0 + t + 1)
                copy(actT[0][:, :, t * P:(t + 1) * P],
                     modv[t % 2][:, :].rearrange("p (c n) -> p c n", c=KC)).then_inc(acthi, 1)

            def finish(l, w):
                b0, nt, (l2, w2) = POST_BASE[(l, w)], POST_TILES[(l, w)], NEXT[(l, w)]
                n0 = NORM_BASE[(l2, w2)]
                for i in range(-1, nt + 1):
                    if i + 1 < nt:
                        t = i + 1
                        if t < nt - 1:
                            act.wait_ge(branch_done, BRANCH_BASE[(l, w)] + t + 1)
                        else:
                            act.wait_ge(unit_used, (U_OUT[l] + N_OUT, U_DN + N_DN)[w])
                        wait(act, psq, b0 + t)
                        act.activation(bjunk[w][:, :].rearrange("p (a n) -> p a n", a=2), ps[:, 2 * t:2 * t + 2, :], ACT.Square,
                                       accum_out=pss[:, t:t + 1]).then_inc(psq, 1)
                    if 0 <= i < nt:
                        act.wait_ge(h_ready, b0 + i + 1)
                        square_h(n0, i)
                    if i >= 1:
                        modulate(l2, w2, i - 1)

            def out_proj(l):
                qt = QTILES[l]
                for t in range(qt):
                    b = 2 * (t % 2)
                    act.wait_ge(mixT, q_base[l] + t + 1)
                    copy(actT[0][:, :, t * P:(t + 1) * P],
                         ps[:, b:b + 2, :].rearrange("p a (c n) -> p (a c) n", c=4)).then_inc(mix_hi, 1)
                for k in range(N_OUT):
                    split_hi(U_OUT[l] + k + 2)
                finish(l, 0)

            def ffn():
                for q in range(FB // 2):
                    u = gu_unit(q)
                    split_hi(u + 2)
                    act.wait_ge(unit_used, u + 1)
                    wait(act, hmul, q)
                    b = gu_bank(q, 0)
                    act.activation(sgate[:, :, :], ps[:, b:b + 2, :], ACT.Silu).then_inc(silu_done, 1)
                    split_hi(u + 3)
                    for half in range(2 if q < MOD_BLOCKS else 0):
                        split_hi(u + 4 + half)

                def upper(f):
                    if f % 2 == 0:
                        wait(act, even_used, f // 2)
                    else:
                        wait(act, unit_used, U_DN + f // 2)
                    copy(hth[f % 2][:, :], hT[f][:, :]).then_inc(hth_ready, 1)

                act.wait_ge(hmul, FB // 2)
                for w in range(N_DN):
                    upper(2 * w)
                    split_hi(U_DN + w + 2)
                    upper(2 * w + 1)
                finish(0, 1)

            def gathered_hi(count):
                act.wait_ge(gv_ready, count)
                copy(xg[0][:, :, :], gv[:, :, :]).then_inc(xg_hi_ready, 1)

            def expert(ee):
                def esplit(k, slot_k, extra):
                    s = slot_k % MRAW
                    act.wait_ge(raw_full[s], ee * (16 * 7) + extra + 16 * (raw_before[s] + slot_k // MRAW))
                    act.wait_ge(unit_used, ee * N_EXP + k + (U_MOE - NSPLIT + 1))
                    copy(whi[slot_k % NSPLIT][:, :], raw[s][:, :]).then_inc(hi_done, 1)

                def silu(units, b):
                    act.wait_ge(unit_used, units)
                    act.wait_ge(e_h, ee * EB + b + 1)
                    act.activation(esg[:, :], ps[:, 0, :], ACT.Silu).then_inc(e_silu, 1)

                def upper(Ts):
                    act.wait_ge(e_T, Ts)
                    copy(ehT[0][:, :, :], ps[:, 2, :].rearrange("p (a n) -> p a n", a=4)).then_inc(e_hi, 1)

                esplit(2, 2, 16)
                esplit(3, 3, 16)
                silu(ee * N_EXP + (U_MOE + 2), 0)
                esplit(4, 4, 16)
                esplit(5, 5, 16)
                with act.Fori(1, EB) as b:
                    esplit(b * 6, 6, b * 16)
                    esplit(b * 6 + 1, 7, b * 16)
                    silu(ee * N_EXP + b * 6 + U_MOE, b)
                    upper(ee * EB + b)
                    for j in range(2, 6):
                        esplit(b * 6 + j, 6 + j, b * 16)
                upper(ee * EB + EB)
                esplit(N_EXP, 0, 16 * 8)
                gathered_hi(ee + 2)
                for hf in range(2):
                    if hf == 0:
                        act.wait_ge(e_down, ee + 1)
                    else:
                        act.wait_ge(unit_used, ee * N_EXP + (U_MOE + N_EXP))
                    act.wait_ge(scat_mm, ee * 2 + 1)
                    copy(ysb[:, hf * 512:(hf + 1) * 512], ps[:, 5 + hf, :]).then_inc(ysb_ready, 1)
                esplit(N_EXP + 1, 1, 16 * 8)

            def program():
                act.wait_ge(cols_ready, 1)
                act.activation(condf[:, :], cols[:, 0:2 * KC], ACT.Silu).then_inc(silu_c, 1)
                for u in range(2):
                    split_hi(u)
                for l in range(DEPTH):
                    for k in range(N_MOD if l == 0 else 0):
                        split_hi(k + 2)
                    if l == 0:
                        first_norm()
                    in_proj(l)
                    mixer(l)
                    out_proj(l)
                    if l == 0:
                        ffn()
                act.wait_ge(wr_ld, 16)
                copy(wrh[:, :, :], wr[:, :, :]).then_inc(wr_hi, 1)
                for k in range(2):
                    act.wait_ge(raw_full[k], 16 * (raw_before[k] + 1))
                    act.wait_ge(unit_used, U_MOE + k - NSPLIT + 1)
                    copy(whi[k][:, :], raw[k][:, :]).then_inc(hi_done, 1)
                act.wait_ge(top_ready, 1)
                act.activation(egap[:, :], gap[:, :], ACT.Exp).then_inc(egap_ready, 1)
                act.nop().then_inc(e_silu, 1)
                gathered_hi(1)
                with act.Fori(0, NE) as e:
                    expert(e + 0)
                act.wait_ge(rank_ready, 1)
                with act.Fori(0, MAX_OVER) as i:
                    more = act.value_load(more_i[0:1, bass.ds(i, 1)], min_val=0, max_val=1)
                    with act.If(more):
                        expert(i + NE)
                    act.nop()
                act.wait_ge(y_done, 1)
                for t in range(LT):
                    wait(act, fsq, t)
                    act.activation(gv[:, :, :].rearrange("p a n -> p (a n)"), y[:, t, :], ACT.Square,
                                   accum_out=pss[:, t:t + 1]).then_inc(fsq, 1)

            program()

        @block.tensor
        def _(pe):
            def mm(o, lhsT, rhs, start=True, stop=True):
                return pe.matmul(o, lhsT, rhs, start=start, stop=stop)

            def mm3(o, a, b, start, stop):
                mm(o, a[0], b[0], start, False)
                mm(o, a[0], b[1], False, False)
                return mm(o, a[1], b[0], False, stop)

            def piece(u):
                pe.wait_ge(lo_done, u + 1)
                return whi[u % NSPLIT], wlo[u % NSPLIT]

            def mod_rows(l, b):
                gb = l * MOD_BLOCKS + b
                bank = gb % 2 if l == 0 else 6
                wait(pe, mrow_ready, gb - 1 + l)
                for half in range(2):
                    w2 = piece(mod_unit(l, b) + half)
                    for k in range(4):
                        for i in range(2):
                            ins = mm(ps[:, bank, :], cond4[:, 4 * half + k, :], w2[i][:, k * 512:(k + 1) * 512],
                                     start=half + k + i == 0, stop=half == 1 and k == 3 and i == 1)
                    ins.then_inc(unit_used, 1)

            def mod_spread(l, b):
                gb = l * MOD_BLOCKS + b
                pe.wait_ge(mrow_ready, gb + 1)
                pe.wait_ge(bmod_ld[mbuf(l, b)], 16 * mbias(l, b))
                m = mrow[mbuf(l, b)]
                for j in range(4):
                    at_ = ((b // 2) * KC + (b % 2) * 4 + j) * 2
                    ins = mm(ps[:, (2, 7)[l], at_:at_ + 2], m[0:5, j * P:(j + 1) * P], K("selcol")[0:5, :])
                ins.then_inc(mod_used, 1)

            def gates(l):
                for i in range(QTILES[l] // LT):
                    for w in range(2):
                        wait(pe, gate_done, gate_base[l] + 2 * i + w - 1)
                        for k in range(KC):
                            ins = mm(ps[:, 4 + 2 * w + k // 4, (k % 4) * P:(k % 4 + 1) * P],
                                     gcol[:, w, i, k:k + 1].broadcast_to([P, P]), ident)
                        ins.then_inc(gate_mm, 1)

            def norm(l, w):
                n0 = NORM_BASE[(l, w)]
                if (l, w) == (0, 0):
                    pe.wait_ge(modc_ready, 1)
                for t in range(NORM_TILES[(l, w)]):
                    pe.wait_ge(xh_ready, n0 + t + 1)
                    for k in range(KC):
                        ins = pe.transpose(ps[:, 2 * t + k // 4, (k % 4) * P:(k % 4 + 1) * P],
                                           xh[t % 2][:, k * P:(k + 1) * P], ident)
                    ins.then_inc(xhT_ready, 1)

            def in_proj(l):
                pe.wait_ge(actlo, NORM_BASE[(l, 0)] + NT)
                for b in range(IN_BLOCKS):
                    for half in range(2):
                        w2 = piece(U_IN[l] + 2 * b + half)
                        if half == 0 and b == 1:
                            gates(l)
                            pe.wait_ge(gate_done, gate_base[l] + QTILES[l])
                        if half == 0 and b >= 2:
                            pe.wait_ge(z_act, l * IN_BLOCKS + b - 1)
                            pe.wait_ge(z_dve, zdve_count(l, b - 2))
                        for t in range(in_tiles(l, b)):
                            for k in range(4):
                                a = [x_[:, 4 * half + k, t * P:(t + 1) * P] for x_ in actT]
                                ins = mm3(ps[:, (b % 2) * 4 + t, 0:IN_W], a, [w_[:, k * IN_W:(k + 1) * IN_W] for w_ in w2],
                                          half + k == 0, half == 1 and k == 3)
                        ins.then_inc(unit_used, 1)

            def mixer(l):
                qt = QTILES[l]
                pe.wait_ge(z_act, IN_BLOCKS * (l + 1))
                pe.wait_ge(z_dve, zdve_count(l, IN_BLOCKS - 1))
                pe.wait_ge(small_ld, 16 * 4 * (l + 1))
                for g in range(4):
                    ins = pe.transpose(ps[:, 0, g * P:(g + 1) * P], sgw[:, g, :], ident)
                ins.then_inc(sgw_T, 1)
                pe.wait_ge(sgw_ready, l + 1)
                for t in range(qt):
                    pe.wait_ge(sv_ready, q_base[l] + t + 1)
                    wait(pe, sgu_out, q_base[l] + t - 1)
                    for g in range(4):
                        ins = mm(ps[:, 1 + t % 2, g * 64:(g + 1) * 64], sgwT[:, g, :],
                                 z[:, t, C_SG + GW + g * 64:C_SG + GW + (g + 1) * 64])
                    ins.then_inc(sgu_mm, 1)
                for s in range(qt // 2):
                    si = s_base[l] + s
                    wait(pe, fU_ready, si)
                    for m in range(2):
                        for k in range(2):
                            ins = mm(ps[:, 3 + m, :], z[:, 2 * s + k, m * P:(m + 1) * P], dft[:, k, :], k == 0, k == 1)
                    ins.then_inc(f1, 1)
                    pe.wait_ge(fU_ready, si + 1)
                    for m in range(2):
                        o = ps[:, 5, m * 256:(m + 1) * 256]
                        mm(o, K("cch"), fU[:, m, 0:256], True, False)
                        ins = mm(o, K("nsch"), fU[:, m, 256:512], False, True)
                    ins.then_inc(f2, 1)
                    pe.wait_ge(fY_ready, si + 1)
                    wait(pe, four_out, si)
                    for k in range(2):
                        for m in range(2):
                            ins = mm(ps[:, 6, k * 256:(k + 1) * 256], fY[:, m, k * P:(k + 1) * P], w_four[:, m, :],
                                     m == 0, m == 1)
                    ins.then_inc(f3, 1)
                pe.wait_ge(rope_done, 2 * (l + 1))
                if l == 0:
                    pe.wait_ge(qctx_ready, NT - LT)
                pe.wait_ge(sgu_out, q_base[l] + qt)
                for t in range(NT):
                    b = 1 + t % 2
                    if t >= 2:
                        pe.wait_ge(winT_out, l * NT + t - 1)
                    q_ = qkr[:, t, 0:256] if t < LT else qctx[:, t - LT, :]
                    k_ = qkr[:, t, 256:384] if t < LT else z[:, t, C_WK:C_WV]
                    if t < qt:
                        for j in range(2):
                            pe.transpose(ps[:, b, j * P:(j + 1) * P], q_[:, j * P:(j + 1) * P], ident)
                    pe.transpose(ps[:, b, 256:384], k_, ident).then_inc(winT, 1)
                for i in range(NT + 2):
                    if i < NT:
                        t = i
                        b = 3 + t % 2
                        pe.wait_ge(mxn, l * NT + t + 1)
                        if t >= 2:
                            pe.wait_ge(mT_out, l * NT + t - 1)
                        if t < qt:
                            for j in range(2):
                                pe.transpose(ps[:, b, j * P:(j + 1) * P], z[:, t, C_CQ + j * P:C_CQ + (j + 1) * P], ident)
                        pe.transpose(ps[:, b, 256:384], z[:, t, C_CKV:C_KR], ident).then_inc(mT, 1)
                    if 1 <= i <= NT:
                        t = i - 1
                        pe.wait_ge(mT_out, l * NT + t + 1)
                        if t == 0:
                            pe.wait_ge(four_out, s_base[l] + qt // 2)
                        else:
                            pe.wait_ge(qkv_out, l * NT + t)
                        if t < qt:
                            for j in range(2):
                                mm(ps[:, 5, 0:384], cqT[:, j, t * P:(t + 1) * P], w_uq[:, j, :], j == 0, j == 1)
                        mm(ps[:, 6, :], ckvT[:, t * P:(t + 1) * P], w_ukv[:, :]).then_inc(qkv_mm, 1)
                    if i >= 2:
                        t = i - 2
                        pe.wait_ge(qkv_out, l * NT + t + 1)
                        if t:
                            pe.wait_ge(mT2_out, l * NT + t)
                        for hh in range(MH):
                            if t < qt:
                                pe.transpose(ps[0:QK, 7, hh * P:(hh + 1) * P], qm[t % 2][:, hh, :], ident)
                            ins = pe.transpose(ps[0:QK, 0, hh * P:(hh + 1) * P], km[t % 2][:, hh, :], ident)
                        ins.then_inc(mT2, 1)
                pe.wait_ge(winT_out, NT * (l + 1))
                pe.wait_ge(mT2_out, NT * (l + 1))
                n = qt * 8
                for i in range(n + 3):
                    if i < n:
                        t, kind, hh = a_units[i]
                        g = att_base[l] + i
                        k0 = 0 if t < LT else LT
                        wait(pe, probs_ready, g - 3)
                        if kind == 0:
                            pr = slice(64 * (hh // 2), 64 * (hh // 2) + 64)
                            mm(ps[:, SCORE[i % 4], 0:(NT - k0) * P], qTw[pr, hh % 2, t * P:(t + 1) * P],
                               kTw[pr, k0 * P:]).then_inc(scores, 1)
                        else:
                            mm(ps[:, SCORE[i % 4], 0:(NT - k0) * P], qTm[0:QK, hh, t * P:(t + 1) * P],
                               kTm[0:QK, hh, k0 * P:]).then_inc(scores, 1)
                    if 2 <= i <= n + 1:
                        j = i - 2
                        g = att_base[l] + j
                        nk = NT if a_units[j][0] < LT else NT - LT
                        pe.wait_ge(probs_ready, g + 1)
                        wait(pe, probT_ready, g - 1)
                        for k in range(nk):
                            ins = pe.transpose(ps[:, 2 + j % 2, k * P:(k + 1) * P], probs[j % 2][:, k * P:(k + 1) * P], ident)
                        ins.then_inc(probs_T, 1)
                    if i >= 3:
                        j = i - 3
                        t, kind, hh = a_units[j]
                        g = att_base[l] + j
                        k0 = 0 if t < LT else LT
                        pe.wait_ge(probT_ready, g + 1)
                        wait(pe, att_out, g - 1)
                        for k in range(k0, NT):
                            v = z[:, k, C_WV + (hh // 2) * HD:C_WV + (hh // 2 + 1) * HD] if kind == 0 else \
                                vm[:, k, hh * HD:(hh + 1) * HD]
                            ins = mm(ps[:, 4 + j % 2, 0:HD], probT[j % 2][:, (k - k0) * P:(k - k0 + 1) * P], v,
                                     k == k0, k == NT - 1)
                        ins.then_inc(pv, 1)

            def out_proj(l):
                qt = QTILES[l]
                pe.wait_ge(att_out, att_base[l] + 8 * qt)
                pe.wait_ge(sgu_out, q_base[l] + qt)
                pe.wait_ge(four_out, s_base[l] + qt // 2)
                for t in range(qt):
                    if t >= 2:
                        pe.wait_ge(mix_lo, q_base[l] + t - 1)
                    for k in range(KC):
                        b = 2 * (t % 2) + k // 4
                        ins = pe.transpose(ps[:, b, (k % 4) * P:(k % 4 + 1) * P],
                                           z[:, t, MIX_COLS[k]:MIX_COLS[k] + P], ident)
                    ins.then_inc(mixT, 1)
                pe.wait_ge(mix_lo, q_base[l] + qt)
                for b in range(2):
                    for half in range(2):
                        w2 = piece(U_OUT[l] + 2 * b + half)
                        for t in range(qt):
                            for k in range(4):
                                a = [x_[:, 4 * half + k, t * P:(t + 1) * P] for x_ in actT]
                                ins = mm3(ps[:, 2 * t + b, :], a, [w_[:, k * 512:(k + 1) * 512] for w_ in w2],
                                          half + k == 0, half == 1 and k == 3)
                            if b + half == 2 and t < qt - 1:
                                ins.then_inc(branch_done, 1)
                        ins.then_inc(unit_used, 1)
                norm(*NEXT[(l, 0)])

            def ffn():
                pe.wait_ge(actlo, NORM_BASE[(0, 1)] + NT)
                for q in range(FB // 2):
                    for i in range(2):
                        w2 = piece(gu_unit(q) + i)
                        last = 2 * q + i - 3
                        if last >= 0:
                            pe.wait_ge((silu_done, hmul)[last % 2], last // 2 + 1)
                        for j in range(2):
                            for k in range(KC):
                                a = [w_[:, k * 256 + j * P:k * 256 + (j + 1) * P] for w_ in w2]
                                ins = mm3(ps[:, gu_bank(q, i) + j, :], a, [x_[:, k, :] for x_ in actT],
                                          k == 0, k == KC - 1)
                        ins.then_inc(unit_used, 1)
                        if i == 0 and 1 <= q <= MOD_BLOCKS:
                            mod_spread(1, q - 1)
                    if q < MOD_BLOCKS:
                        if q == 0:
                            pe.wait_ge(cond_ready, 2)
                        mod_rows(1, q)
                pe.wait_ge(modc_ready, 2)
                pe.wait_ge(hmul, FB // 2)
                for w in range(N_DN):
                    w2 = piece(U_DN + w)
                    for i in range(2):
                        f = 2 * w + i
                        pe.wait_ge(htl_ready, f + 1)
                        for t in range(NT):
                            for hf in range(2):
                                a = [hth[f % 2][:, t * P:(t + 1) * P], htl[f % 2][:, t * P:(t + 1) * P]]
                                ins = mm3(ps[:, 2 * t + hf, :], a,
                                          [w_[:, i * D + hf * 512:i * D + (hf + 1) * 512] for w_ in w2], f == 0, f == FB - 1)
                            if f == FB - 1 and t < NT - 1:
                                ins.then_inc(branch_done, 1)
                        ins.then_inc((even_used, unit_used)[i], 1)
                norm(*NEXT[(0, 1)])

            def router():
                pe.wait_ge(actlo, NORM_BASE[(1, 1)] + LT)
                pe.wait_ge(wr_ready, 1)
                for t in range(LT):
                    for k in range(KC):
                        for i in range(2):
                            for j in range(2):
                                ins = mm(ps[:, 4, t * NE:(t + 1) * NE], actT[i][:, k, t * P:(t + 1) * P],
                                         (wrh, wrl)[j][:, k, :], k + i + j == 0, k == KC - 1 and i + j == 2)
                ins.then_inc(logits_mm, 1)
                pe.wait_ge(chosen_ready, 1)
                mm(ps[:, 5, 0:NE], K("before"), chosen[:, 0, :])
                mm(ps[:, 5, NE:2 * NE], K("before"), chosen[:, 1, :], True, False)
                mm(ps[:, 5, NE:2 * NE], K("ones"), chosen[:, 0, :], False, True)
                mm(ps[:, 5, 2 * NE:3 * NE], K("ones"), chosen[:, 0, :], True, False)
                mm(ps[:, 5, 2 * NE:3 * NE], K("ones"), chosen[:, 1, :], False, True).then_inc(rank_mm, 1)

            def gather(count):
                pe.wait_ge(pick_ready, count)
                for k in range(KC):
                    for t in range(LT):
                        ins = mm(ps[:, 3 + k // 4, (k % 4) * P:(k % 4 + 1) * P], xh[t][:, k * P:(k + 1) * P],
                                 pick[:, t, :], t == 0, t == LT - 1)
                ins.then_inc(gather_mm, 1)

            def expert(ee):
                def gate_up(us, slot_k, bank, sm, b):
                    for half in range(2):
                        pe.wait_ge(lo_done, us + (half + 1))
                        if half == 0:
                            pe.wait_ge(sm, ee * EB + b + 1)
                        s = (slot_k + half) % NSPLIT
                        for k in range(4):
                            ins = mm3(ps[:, bank, :], [g_[:, 4 * half + k, :] for g_ in xg],
                                      [w_[s][:, k * 512:(k + 1) * 512] for w_ in (whi, wlo)],
                                      half + k == 0, half == 1 and k == 3)
                        ins.then_inc(unit_used, 1)

                def turn(b):
                    pe.wait_ge(e_h, ee * EB + b + 1)
                    pe.wait_ge(e_lo, ee * EB + b)
                    for k in range(4):
                        ins = pe.transpose(ps[:, 2, k * P:(k + 1) * P], eh[:, k * P:(k + 1) * P], ident)
                    ins.then_inc(e_T, 1)

                def down_part(slot_k, half, k, hf, start, stop):
                    s = (slot_k + half) % NSPLIT
                    return mm3(ps[:, 5 + hf, :], [h_[:, 2 * half + k, :] for h_ in ehT],
                               [w_[s][:, k * D + hf * 512:k * D + (hf + 1) * 512] for w_ in (whi, wlo)], start, stop)

                def step(b, first):
                    gate_up(base + (b * 6 - 2), 4, 0, e_silu, b)
                    turn(b)
                    gate_up(base + b * 6, 6, 1, e_h, b)
                    pe.wait_ge(e_lo, ee * EB + b + 1)
                    for half in range(2):
                        pe.wait_ge(lo_done, base + (b * 6 + (3 + half)))
                        for k in range(2):
                            for hf in range(2):
                                ins = down_part(8, half, k, hf, first and half + k == 0, False)
                        ins.then_inc(unit_used, 1)

                base = ee * N_EXP + U_MOE
                pe.wait_ge(xg_ready, ee + 1)
                gate_up(base, 0, 0, e_silu, 0)
                gate_up(base + 2, 2, 1, e_h, 0)
                pe.wait_ge(y_added, ee + 1)
                for t in range(LT):
                    ins = pe.transpose(ps[:, 7, t * P:(t + 1) * P], pick[:, t, :], ident)
                ins.then_inc(pickT_mm, 1)
                step(1, True)
                with pe.Fori(2, EB) as b:
                    step(b, False)
                turn(EB)
                gather(ee + 2)
                pe.wait_ge(e_lo, ee * EB + (EB + 1))
                pe.wait_ge(lo_done, base + N_EXP)
                for hf in range(2):
                    for half in range(2):
                        for k in range(2):
                            ins = down_part(40, half, k, hf, False, half + k == 2)
                        if hf == 1:
                            ins.then_inc(unit_used, 1)
                    if hf == 0:
                        ins.then_inc(e_down, 1)
                pe.wait_ge(pickT_ready, ee + 1)
                pe.wait_ge(gv_ready, ee + 2)
                for hf in range(2):
                    pe.wait_ge(ysb_ready, ee * 2 + (1 + hf))
                    for t in range(LT):
                        ins = mm(ps[:, SCAT[2 * t + hf], :], pickT[:, t, :], ysb[:, hf * 512:(hf + 1) * 512])
                    ins.then_inc(scat_mm, 1)

            def program():
                pe.wait_ge(con_ld, 16)
                pe.wait_ge(cond_ld, 32)
                pe.wait_ge(rows_ld, 16 * 5)
                pe.transpose(ps[:, 0, 0:NROWS], rows[0:NROWS, :], ident[0:NROWS, 0:NROWS]).then_inc(rows_T, 1)
                for l in range(DEPTH):
                    if l == 0:
                        pe.wait_ge(cond_ready, 1)
                        for b in range(MOD_BLOCKS + 1):
                            if b < MOD_BLOCKS:
                                mod_rows(0, b)
                            if b:
                                mod_spread(0, b - 1)
                    if l == 0:
                        norm(0, 0)
                    in_proj(l)
                    mixer(l)
                    out_proj(l)
                    if l == 0:
                        ffn()
                router()
                pe.nop().then_inc(scat_mm, 1)
                gather(1)
                with pe.Fori(0, NE) as e:
                    expert(e + 0)
                pe.wait_ge(rank_ready, 1)
                with pe.Fori(0, MAX_OVER) as i:
                    more = pe.value_load(more_i[0:1, bass.ds(i, 1)], min_val=0, max_val=1)
                    with pe.If(more):
                        expert(i + NE)
                    pe.nop()

            program()

        @block.vector
        def _(dve):
            chain = [0]

            def link(ins):
                chain[0] += 1
                ins.then_inc(dve_c, 1)
                dve.wait_ge(dve_c, chain[0])

            def split_lo(u):
                if u >= U_MOE:
                    return
                n = 4 * IN_W if U_IN[0] <= u < U_OUT[0] or U_IN[1] <= u < U_OUT[1] else UNIT
                dve.wait_ge(hi_done, u + 1)
                sub(wlo[u % NSPLIT][:, 0:n], raw[u % NRAW][:, 0:n], whi[u % NSPLIT][:, 0:n]).then_inc(lo_done, 1)

            def sub(o, a, b):
                return dve.tensor_tensor(o, a, b.bitcast(F32), ALU.subtract)

            def cond_parts():
                cf = condf[:, :].rearrange("p (s c) -> p c s", s=2)
                link(dve.memset(cond4[:, :, :].bitcast(F32), 0.0))
                link(dve.tensor_copy(cond4[:, :, 0:2], cf))
                sub(cond4[:, :, 2:4], cf, cond4[:, :, 0:2]).then_inc(cond_ready, 1)

            def mod_block(l, b):
                gb = l * MOD_BLOCKS + b
                bank = gb % 2 if l == 0 else 6
                dve.wait_ge(unit_used, mod_unit(l, b) + 2)
                wait(dve, mod_used, gb - 1 + l)
                dve.tensor_copy(mrow[mbuf(l, b)][0:4, :], ps[0:4, bank, :]).then_inc(mrow_ready, 1)

            def mod_columns(l):
                dve.wait_ge(mod_used, (l + 1) * MOD_BLOCKS)
                mc = ps[:, (2, 7)[l], 0:96].rearrange("p (v k i) -> p v i k", v=6, i=2)
                for w in range(2):
                    for i in range(2):
                        r = (R_PRE_MIX, R_PRE_FFN)[w] + l * KC
                        dve.scalar_tensor_tensor(out=acol[:, w, i, :], in0=mc[:, 3 * w + 1, i, :], scalar=1.0,
                                                 in1=cols[:, r:r + KC], op0=ALU.add, op1=ALU.mult)
                        dve.tensor_copy(bcol[:, w, i, :], mc[:, 3 * w, i, :])
                        ins = dve.tensor_copy(gcol[:, w, i, :], mc[:, 3 * w + 2, i, :])
                ins.then_inc(modc_ready, 1)
                dve.wait_ge(modc_ready, l + 1)

            def gates(l):
                dve.wait_ge(gpost_ld, 16 * (4 if l == 0 else 6))
                for i in range(QTILES[l] // LT):
                    for w in range(2):
                        dve.wait_ge(gate_mm, gate_base[l] + 2 * i + w + 1)
                        for hf in range(2):
                            g_ = (gate_a, gate_f)[w][:, i, hf * 512:(hf + 1) * 512]
                            ins = dve.tensor_tensor(g_, ps[:, 4 + 2 * w + hf, :], g_, ALU.mult)
                        ins.then_inc(gate_done, 1)

            def modulated(dst, src, w, i):
                for k in range(KC):
                    ins = dve.tensor_scalar(dst[:, k * P:(k + 1) * P], src[:, k, :], acol[:, w, i, k:k + 1],
                                            bcol[:, w, i, k:k + 1], ALU.mult, ALU.add)
                return ins

            def norm_var(n0, t):
                dve.wait_ge(sq_done, n0 + t + 1)
                dve.tensor_scalar(var[:, t:t + 1], ss[:, t:t + 1], 1.0 / D, EPS, ALU.mult, ALU.add).then_inc(var_ready, 1)

            def norm_scale(n0, t):
                dve.wait_ge(rstd_ready, n0 + t + 1)
                if t >= 2:
                    dve.wait_ge(xhT_ready, n0 + t - 1)
                dve.tensor_scalar(xh[t % 2][:, :], h[:, t, :], rstd[:, t:t + 1], None, ALU.mult).then_inc(xh_ready, 1)

            def norm_lo(n0, t):
                dve.wait_ge(acthi, n0 + t + 1)
                sub(actT[1][:, :, t * P:(t + 1) * P], modv[t % 2][:, :].rearrange("p (c n) -> p c n", c=KC),
                    actT[0][:, :, t * P:(t + 1) * P]).then_inc(actlo, 1)

            def first_norm():
                for t in range(NT):
                    norm_var(0, t)
                for i in range(NT + 1):
                    if i < NT:
                        norm_scale(0, i)
                    if i:
                        norm_lo(0, i - 1)

            def finish(l, w):
                b0, nt, n0 = POST_BASE[(l, w)], POST_TILES[(l, w)], NORM_BASE[NEXT[(l, w)]]
                gate = (gate_a, gate_f)[w]
                for i in range(-1, nt + 2):
                    if i + 1 < nt:
                        t = i + 1
                        dve.wait_ge(psq, b0 + t + 1)
                        dve.tensor_scalar(pvar[:, t:t + 1], pss[:, t:t + 1], 1.0 / D, EPS, ALU.mult,
                                          ALU.add).then_inc(pvar_ready, 1)
                    if 0 <= i < nt:
                        dve.wait_ge(prstd_ready, b0 + i + 1)
                        link(dve.scalar_tensor_tensor(out=ptmp[:, :].rearrange("p (a n) -> p a n", a=2),
                                                      in0=ps[:, 2 * i:2 * i + 2, :], scalar=prstd[:, i:i + 1],
                                                      in1=gate[:, i // LT, :].rearrange("p (a n) -> p a n", a=2),
                                                      op0=ALU.mult, op1=ALU.mult))
                        dve.tensor_tensor(h[:, i, :], h[:, i, :], ptmp[:, :], ALU.add).then_inc(h_ready, 1)
                    if 1 <= i <= nt:
                        norm_scale(n0, i - 1)
                    if 0 <= i < nt:
                        norm_var(n0, i)
                    if i >= 2:
                        norm_lo(n0, i - 2)

            def in_proj(l):
                for b in range(IN_BLOCKS):
                    for half in range(2):
                        split_lo(U_IN[l] + 2 * b + half + 2)
                    if b == 0:
                        gates(l)
                    if in_tiles(l, b) == NT:
                        dve.wait_ge(unit_used, U_IN[l] + 2 * b + 2)
                        for t in range(LT, NT):
                            ins = dve.tensor_copy(z[:, t, b * IN_W:(b + 1) * IN_W], ps[:, (b % 2) * 4 + t, 0:IN_W])
                        ins.then_inc(z_dve, 1)

            def turn(xe, xo, cs, sn, s4):
                dve.tensor_tensor(s4[0], xe, cs, ALU.mult)
                dve.tensor_tensor(s4[1], xo, sn, ALU.mult)
                dve.tensor_tensor(s4[2], xe, sn, ALU.mult)
                link(dve.tensor_tensor(s4[3], xo, cs, ALU.mult))

            def rotate(oe, oo, xe, xo, cs, sn, s4):
                turn(xe, xo, cs, sn, s4)
                dve.tensor_tensor(oe, s4[0], s4[1], ALU.subtract)
                return dve.tensor_tensor(oo, s4[2], s4[3], ALU.add)

            def pairs(ap, heads, n):
                v = ap.rearrange("p (h n i) -> p i h n", h=heads, i=2)
                return v[:, 0, :, :], v[:, 1, :, :]

            def scratch(heads, n):
                return [s_[:, 0:heads * n].rearrange("p (h n) -> p h n", h=heads) for s_ in rope_s]

            def table(name, t, n, heads):
                return rot(name, t, n).unsqueeze(1).broadcast_to([P, heads, n])

            def mixer(l):
                qt = QTILES[l]
                dve.wait_ge(z_act, IN_BLOCKS * (l + 1))
                dve.wait_ge(z_dve, zdve_count(l, IN_BLOCKS - 1))
                for t in range(LT):
                    xe, xo = pairs(z[:, t, C_WQ:C_WV], 6, 32)
                    turn(xe, xo, table("cosw", t, 32, 6), table("sinw", t, 32, 6), scratch(6, 32))
                    for i, op in ((0, ALU.subtract), (1, ALU.add)):
                        s_ = [r_[:, 0:128].rearrange("p (a b n) -> p a b n", a=2, b=2) for r_ in rope_s[2 * i:2 * i + 2]]
                        o = qkr[:, t, 0:256].rearrange("p (b a n i) -> p i a b n", a=2, b=2, i=2)[:, i, :, :, :]
                        dve.tensor_tensor(o, s_[0], s_[1], op)
                        s_ = [r_[:, 128:192].rearrange("p (h n) -> p h n", h=2) for r_ in rope_s[2 * i:2 * i + 2]]
                        ins = dve.tensor_tensor(pairs(qkr[:, t, 256:384], 2, 32)[i], s_[0], s_[1], op)
                    link(ins)
                    xe, xo = pairs(z[:, t, C_KR:C_SG], 1, 16)
                    oe, oo = pairs(krr[:, t, :], 1, 16)
                    ins = rotate(oe, oo, xe, xo, table("cosm", t, 16, 1), table("sinm", t, 16, 1), scratch(1, 16))
                    link(ins)
                    dve.engine_nop().then_inc(rope_done, 1)
                for t in range(LT, qt):
                    dve.tensor_copy(qctx[:, t - LT, :].rearrange("p (b a n) -> p a b n", a=2, b=2),
                                    z[:, t, C_WQ:C_WK].rearrange("p (a b n) -> p a b n", a=2, b=2)).then_inc(qctx_ready, 1)
                dve.wait_ge(sgw_T, l + 1)
                dve.tensor_copy(sgwT[:, :, :], ps[:, 0, :].rearrange("p (g q) -> p g q", g=4)).then_inc(sgw_ready, 1)
                dve.wait_ge(gelu_done, q_base[l] + qt)
                for t in range(qt):
                    ins = dve.bn_stats(bst[:, t, :], z[:, t, C_SG + GW:DIN])
                link(ins)
                for t in range(qt):
                    ins = dve.bn_aggr(mv[:, t, :], bst[:, t, :])
                link(ins)
                dve.tensor_scalar(svar[:, 0:qt], mv[:, 0:qt, 1], EPS, None, ALU.add).then_inc(svar_ready, 1)
                dve.wait_ge(msq, (2 * NT, 2 * NT + NT + LT)[l])
                dve.tensor_scalar(mvar[:, :, 0], mss[:, :, 0], 1.0 / 256, EPS, ALU.mult, ALU.add)
                dve.tensor_scalar(mvar[:, :, 1], mss[:, :, 1], 1.0 / 128, EPS, ALU.mult, ALU.add).then_inc(mvar_ready, 1)
                dve.wait_ge(srstd_ready, l + 1)
                for t in range(qt):
                    v = z[:, t, C_SG + GW:DIN]
                    dve.tensor_scalar(v, v, mv[:, t, 0:1], srstd[:, t:t + 1], ALU.subtract, ALU.mult).then_inc(sv_ready, 1)
                for t in range(qt):
                    dve.wait_ge(sgu_mm, q_base[l] + t + 1)
                    for g in range(4):
                        u = z[:, t, C_SG + g * 64:C_SG + (g + 1) * 64]
                        r = R_SGB + 4 * l + g
                        ins = dve.scalar_tensor_tensor(out=u, in0=ps[:, 1 + t % 2, g * 64:(g + 1) * 64],
                                                       scalar=cols[:, r:r + 1], in1=u, op0=ALU.add, op1=ALU.mult)
                    ins.then_inc(sgu_out, 1)
                dve.wait_ge(mrstd_ready, l + 1)
                for t in range(NT):
                    if t < qt:
                        v = z[:, t, C_CQ:C_CKV]
                        dve.tensor_scalar(v, v, mrstd[:, t, 0:1], None, ALU.mult)
                    v = z[:, t, C_CKV:C_KR]
                    dve.tensor_scalar(v, v, mrstd[:, t, 1:2], None, ALU.mult).then_inc(mxn, 1)
                for s in range(qt // 2):
                    si = s_base[l] + s
                    dve.wait_ge(f2, si + 1)
                    wait(dve, f3, si)
                    dve.tensor_copy(fY[:, :, :], ps[:, 5, :].rearrange("p (m n) -> p m n", m=2)).then_inc(fY_ready, 1)
                for t in range(NT):
                    ai = l * NT + t
                    dve.wait_ge(qkv_mm, ai + 1)
                    wait(dve, mT2, ai - 1)
                    if t < qt:
                        src = ps[:, 5, 0:384].rearrange("p (h n) -> p h n", h=MH)
                        q_ = qm[t % 2]
                        dve.tensor_copy(q_[:, :, 0:NOPE], src[:, :, 0:NOPE])
                        if t < LT:
                            v = src[:, :, NOPE:QK].rearrange("p h (n i) -> p i h n", i=2)
                            o = q_[:, :, NOPE:QK].rearrange("p h (n i) -> p i h n", i=2)
                            link(rotate(o[:, 0, :, :], o[:, 1, :, :], v[:, 0, :, :], v[:, 1, :, :],
                                        table("cosm", t, 16, MH), table("sinm", t, 16, MH), scratch(MH, 16)))
                        else:
                            dve.tensor_copy(q_[:, :, NOPE:QK], src[:, :, NOPE:QK])
                    src = ps[:, 6, :].rearrange("p (h n) -> p h n", h=MH)
                    kr = (krr[:, t, :] if t < LT else z[:, t, C_KR:C_SG]).unsqueeze(1).broadcast_to([P, MH, ROT])
                    dve.tensor_copy(km[t % 2][:, :, 0:NOPE], src[:, :, 0:NOPE])
                    dve.tensor_copy(km[t % 2][:, :, NOPE:QK], kr)
                    dve.tensor_copy(vm[:, t, :].rearrange("p (h n) -> p h n", h=MH), src[:, :, NOPE:]).then_inc(qkv_out, 1)
                n = qt * 8
                for i in range(n + 3):
                    if i < n:
                        t, kind, hh = a_units[i]
                        g = att_base[l] + i
                        nk = NT if t < LT else NT - LT
                        c2 = slice(i % 4, i % 4 + 1)
                        dve.wait_ge(scores, g + 1)
                        wait(dve, probs_ready, g - 3)
                        if kind == 0 and t < LT:
                            o = ps[:, SCORE[i % 4], (1 - t) * P:(2 - t) * P]
                            link(dve.tensor_tensor(o, o, maskv[:, t, :], ALU.add))
                        if kind == 0:
                            link(dve.tensor_reduce(nmx2[:, c2], ps[:, SCORE[i % 4], 0:nk * P], AXX, ALU.max, negate=True))
                            dve.tensor_tensor(nmax[:, c2], nmx2[:, c2], nsink[:, l * WH + hh:l * WH + hh + 1],
                                              ALU.min).then_inc(smax, 1)
                        else:
                            dve.tensor_reduce(nmax[:, c2], ps[:, SCORE[i % 4], 0:nk * P], AXX, ALU.max,
                                              negate=True).then_inc(smax, 1)
                    if i >= 3:
                        j = i - 3
                        t, kind, hh = a_units[j]
                        g = att_base[l] + j
                        c2 = slice(j % 4, j % 4 + 1)
                        dve.wait_ge(probs_ready, g + 1)
                        if kind == 0:
                            link(dve.tensor_tensor(rtot[:, c2], rsum[:, c2], esink[:, c2], ALU.add))
                            link(dve.reciprocal(rinv[:, c2], rtot[:, c2]))
                        else:
                            link(dve.reciprocal(rinv[:, c2], rsum[:, c2]))
                        dve.wait_ge(pv, g + 1)
                        base = (C_WQ, C_CQ)[kind] + hh * HD
                        dve.tensor_scalar(z[:, t, base:base + HD], ps[:, 4 + j % 2, 0:HD], rinv[:, c2], None,
                                          ALU.mult).then_inc(att_out, 1)

            def out_proj(l):
                qt = QTILES[l]
                for t in range(qt):
                    b = 2 * (t % 2)
                    dve.wait_ge(mix_hi, q_base[l] + t + 1)
                    sub(actT[1][:, :, t * P:(t + 1) * P], ps[:, b:b + 2, :].rearrange("p a (c n) -> p (a c) n", c=4),
                        actT[0][:, :, t * P:(t + 1) * P]).then_inc(mix_lo, 1)
                for k in range(N_OUT):
                    split_lo(U_OUT[l] + k + 2)
                finish(l, 0)

            def ffn():
                cond_parts()
                for q in range(FB // 2):
                    u = gu_unit(q)
                    split_lo(u + 2)
                    split_lo(u + 3)
                    dve.wait_ge(unit_used, u + 2)
                    dve.wait_ge(silu_done, q + 1)
                    b = gu_bank(q, 1)
                    for j in range(2):
                        ins = dve.tensor_tensor(hT[2 * q + j][:, :], ps[:, b + j, :], sgate[:, j, :], ALU.mult)
                    ins.then_inc(hmul, 1)
                    if q < MOD_BLOCKS:
                        for half in range(2):
                            split_lo(u + 4 + half)
                        mod_block(1, q)
                    if q == MOD_BLOCKS:
                        mod_columns(1)

                def lower(f):
                    dve.wait_ge(hth_ready, f + 1)
                    sub(htl[f % 2][:, :], hT[f][:, :], hth[f % 2][:, :]).then_inc(htl_ready, 1)

                for w in range(N_DN):
                    lower(2 * w)
                    split_lo(U_DN + w + 2)
                    lower(2 * w + 1)
                finish(0, 1)

            def router():
                dve.wait_ge(wr_hi, 1)
                sub(wrl[:, :, :], wr[:, :, :], wrh[:, :, :]).then_inc(wr_ready, 1)
                dve.wait_ge(logits_mm, 1)
                link(dve.tensor_copy(logit[:, :, :], ps[:, 4, 0:LT * NE].rearrange("p (t n) -> p t n", t=LT)))
                for t in range(LT):
                    ins = dve.max(top8[:, t, :], logit[:, t, :])
                link(ins)
                for t in range(LT):
                    ins = dve.max_index(idx8[:, t, :], top8[:, t, :], logit[:, t, :])
                link(ins)
                dve.tensor_tensor(gap[:, :], top8[:, :, 1], top8[:, :, 0], ALU.subtract).then_inc(top_ready, 1)
                link(dve.tensor_copy(idxf[:, :, :], idx8[:, :, :]))
                for t in range(LT):
                    for i in range(2):
                        ins = dve.tensor_scalar(hot[:, t, i, :], K("iota8"), idxf[:, t, i:i + 1], None, ALU.is_equal)
                link(ins)
                dve.tensor_tensor(chosen[:, :, :], hot[:, :, 0, :], hot[:, :, 1, :], ALU.add).then_inc(chosen_ready, 1)
                dve.wait_ge(egap_ready, 1)
                link(dve.tensor_scalar(eden[:, :], egap[:, :], 1.0, None, ALU.add))
                link(dve.reciprocal(top_w[:, :, 0], eden[:, :]))
                link(dve.tensor_tensor(top_w[:, :, 1], egap[:, :], top_w[:, :, 0], ALU.mult))
                for t in range(LT):
                    ins = dve.tensor_scalar(cmb0[:, t, :], hot[:, t, 0, :], top_w[:, t, 0:1], None, ALU.mult)
                link(ins)
                for t in range(LT):
                    ins = dve.scalar_tensor_tensor(out=weight_of[:, t, 0:NE], in0=hot[:, t, 1, :], scalar=top_w[:, t, 1:2],
                                                   in1=cmb0[:, t, :], op0=ALU.mult, op1=ALU.add)
                dve.wait_ge(chosen_ready, 1)
                link(dve.tensor_scalar(away[:, :, :], chosen[:, :, :], -4096.0, 4096.0, ALU.mult, ALU.add))
                dve.wait_ge(rank_mm, 1)
                link(dve.memset(slot_of[:, :, NR - 1:NR], -1.0))
                link(dve.tensor_tensor(slot_of[:, :, 0:NE], ps[:, 5, 0:LT * NE].rearrange("p (t n) -> p t n", t=LT),
                                       away[:, :, :], ALU.add))
                choose(0)
                link(dve.tensor_scalar(over8[:, :], ps[:, 5, LT * NE:(LT + 1) * NE], float(P), None, ALU.is_gt))
                link(dve.tensor_tensor(more_f[:, :], over8[:, :], K("left8"), ALU.mult))
                link(dve.max(more8[:, :], more_f[:, :]))
                dve.tensor_scalar(more_i[:, :], more8[:, :], 0.5, None, ALU.is_gt)
                link(dve.tensor_scalar(more_f[:, :], more8[:, :], -1.0, float(NE), ALU.mult, ALU.add))
                link(dve.tensor_scalar(more_f[:, :], more_f[:, :], float(NE - 1), None, ALU.min))
                dve.tensor_copy(round_e[:, 0:NE], K("iota8"))
                dve.tensor_copy(round_e[:, NE:NR], more_f[:, 0:NR - NE])
                dve.tensor_scalar(rank1[:, :, :], slot_of[:, :, 0:NE], -float(P), None, ALU.add)
                link(dve.tensor_tensor(late[:, :, :], K("iota8").unsqueeze(1).broadcast_to([P, MAX_OVER, NE]),
                                       more_f[:, 0:MAX_OVER].unsqueeze(2).broadcast_to([P, MAX_OVER, NE]),
                                       ALU.is_equal))
                for t in range(LT):
                    for o, v in ((late_r, rank1[:, t, :]), (late_w, weight_of[:, t, 0:NE])):
                        ins = dve.tensor_tensor(o[:, t, :, :], late[:, :, :],
                                                v.unsqueeze(1).broadcast_to([P, MAX_OVER, NE]), ALU.mult)
                link(ins)
                link(dve.tensor_reduce(slot_of[:, :, NE:NR - 1], late_r[:, :, :, :], AXX, ALU.add))
                link(dve.tensor_reduce(weight_of[:, :, NE:NR - 1], late_w[:, :, :, :], AXX, ALU.add))
                dve.engine_nop().then_inc(rank_ready, 1)
                dve.memset(y[:, :, :], 0.0).then_inc(y_added, 1)
                dve.engine_nop().then_inc(e_h, 1)
                dve.engine_nop().then_inc(e_lo, 1)

            def choose(r):
                for t in range(LT):
                    ins = dve.tensor_scalar(pick[:, t, :], K("iota"), slot_of[:, t, bass.ds(r, 1)], None, ALU.is_equal)
                ins.then_inc(pick_ready, 1)

            def gathered(count):
                dve.wait_ge(gather_mm, count)
                modulated(gv[:, :, :].rearrange("p c n -> p (c n)"),
                          ps[:, 3:5, :].rearrange("p a (c n) -> p (a c) n", c=4), 1, 0).then_inc(gv_ready, 1)

            def gathered_lo(count):
                dve.wait_ge(xg_hi_ready, count)
                sub(xg[1][:, :, :], gv[:, :, :], xg[0][:, :, :]).then_inc(xg_ready, 1)

            def expert(ee):
                def esplit(k, slot_k):
                    dve.wait_ge(hi_done, ee * N_EXP + k + (U_MOE + 1))
                    sub(wlo[slot_k % NSPLIT][:, :], raw[slot_k % MRAW][:, :],
                        whi[slot_k % NSPLIT][:, :]).then_inc(lo_done, 1)

                def lower(count):
                    dve.wait_ge(e_hi, count)
                    sub(ehT[1][:, :, :], ps[:, 2, :].rearrange("p (a n) -> p a n", a=4),
                        ehT[0][:, :, :]).then_inc(e_lo, 1)

                def hidden(units, b):
                    dve.wait_ge(unit_used, units)
                    dve.wait_ge(e_silu, ee * EB + b + 2)
                    dve.tensor_tensor(eh[:, :], ps[:, 1, :], esg[:, :], ALU.mult).then_inc(e_h, 1)

                base = ee * N_EXP + U_MOE
                for k in range(2, 6):
                    esplit(k, k)
                hidden(base + 4, 0)
                dve.wait_ge(pickT_mm, ee + 1)
                dve.tensor_copy(pickT[:, :, :], ps[:, 7, 0:LT * P].rearrange("p (t n) -> p t n", t=LT)).then_inc(pickT_ready, 1)
                choose(ee + 1)
                with dve.Fori(1, EB) as b:
                    esplit(b * 6, 6)
                    esplit(b * 6 + 1, 7)
                    lower(ee * EB + b)
                    esplit(b * 6 + 2, 8)
                    esplit(b * 6 + 3, 9)
                    hidden(base + (b * 6 + 2), b)
                    esplit(b * 6 + 4, 10)
                    esplit(b * 6 + 5, 11)
                lower(ee * EB + EB)
                esplit(N_EXP, 0)
                gathered(ee + 2)
                gathered_lo(ee + 2)
                esplit(N_EXP + 1, 1)
                dve.wait_ge(y_added, ee + 1)
                for hf in range(2):
                    dve.wait_ge(scat_mm, ee * 2 + (2 + hf))
                    for t in range(LT):
                        o = y[:, t, hf * 512:(hf + 1) * 512]
                        ins = dve.scalar_tensor_tensor(out=o, in0=ps[:, SCAT[2 * t + hf], :],
                                                       scalar=weight_of[:, t, bass.ds(ee, 1)], in1=o,
                                                       op0=ALU.mult, op1=ALU.add)
                ins.then_inc(y_added, 1)

            def program():
                dve.memset(mhalf[:, :], -0.5)
                link(dve.memset(mss[:, :, :], 1.0))
                dve.wait_ge(sink_ld, 16)
                dve.tensor_scalar(nsink[:, :], sinks[:, :], -1.0, None, ALU.mult)
                dve.wait_ge(rows_T, 1)
                dve.tensor_copy(cols[:, 0:NROWS], ps[:, 0, 0:NROWS]).then_inc(cols_ready, 1)
                dve.wait_ge(silu_c, 1)
                for u in range(2):
                    split_lo(u)
                for l in range(DEPTH):
                    if l == 0:
                        cond_parts()
                        for b in range(MOD_BLOCKS):
                            split_lo(2 * b + 2)
                            split_lo(2 * b + 3)
                            mod_block(0, b)
                        mod_columns(0)
                    if l == 0:
                        first_norm()
                    in_proj(l)
                    mixer(l)
                    out_proj(l)
                    if l == 0:
                        ffn()
                router()
                gathered(1)
                for k in range(2):
                    dve.wait_ge(hi_done, U_MOE + k + 1)
                    sub(wlo[k][:, :], raw[k][:, :], whi[k][:, :]).then_inc(lo_done, 1)
                gathered_lo(1)
                with dve.Fori(0, NE) as e:
                    expert(e + 0)
                dve.wait_ge(rank_ready, 1)
                with dve.Fori(0, MAX_OVER) as i:
                    more = dve.value_load(more_i[0:1, bass.ds(i, 1)], min_val=0, max_val=1)
                    with dve.If(more):
                        expert(i + NE)
                    dve.engine_nop()
                dve.engine_nop().then_inc(y_done, 1)
                dve.wait_ge(fsq, LT)
                dve.tensor_scalar(pvar[:, 0:LT], pss[:, 0:LT], 1.0 / D, EPS, ALU.mult, ALU.add).then_inc(fvar, 1)
                dve.wait_ge(frstd, 1)
                for t in range(LT):
                    link(dve.scalar_tensor_tensor(out=y[:, t, :], in0=y[:, t, :], scalar=prstd[:, t:t + 1],
                                                  in1=gate_f[:, 0, :], op0=ALU.mult, op1=ALU.mult))
                    dve.tensor_tensor(h[:, t, :], h[:, t, :], y[:, t, :], ALU.add).then_inc(fin, 1)

            program()


def gu_bank(q, i):
    return 2 * ((2 * q + i) % 3)


SCORE = [0, 1, 6, 7]
SCAT = [7, 3, 4, 2]


def shape_constants():
    t = {}
    i = np.arange(P)
    t["ident"] = np.eye(P)
    n = np.arange(SEQ)
    ang = 2 * np.pi * (np.outer(n, n) % SEQ) / SEQ
    cs = np.concatenate([np.cos(ang), np.sin(ang)], axis=1).reshape(2, P, 2 * SEQ)
    t["dft"] = cs.transpose(1, 0, 2).reshape(P, -1)
    ch = GW // 4
    m = np.arange(ch)
    ang = 2 * np.pi * (np.outer(m, m) % ch) / ch
    scale = (SEQ * ch) ** -0.5
    t["cch"] = np.kron(np.eye(2), np.cos(ang)) * scale
    t["nsch"] = -np.kron(np.eye(2), np.sin(ang)) * scale
    q, k = np.meshgrid(i, i, indexing="ij")
    masks = []
    for tile in range(2):
        far = np.abs((k + (1 - tile) * P) - (q + tile * P)) > WINDOW
        masks.append(np.where(far, -1e30, 0.0))
    t["mask"] = np.concatenate(masks, axis=1)
    for suffix, dim in (("w", HD), ("m", ROT)):
        nf = dim // 4
        inv = (np.float32(10000.0) ** (-np.arange(nf, dtype=np.float32) / nf)).astype(np.float32)
        row = np.repeat(np.arange(SEQ // GRID_W, dtype=np.float32), GRID_W)
        col = np.tile(np.arange(GRID_W, dtype=np.float32), SEQ // GRID_W)
        a = np.concatenate([row[:, None] * inv, col[:, None] * inv], axis=-1).astype(np.float64)
        for fn, nm in ((np.cos, "cos"), (np.sin, "sin")):
            t[nm + suffix] = fn(a).reshape(2, P, -1).transpose(1, 0, 2).reshape(P, -1)
    t["iota"] = np.tile(i[None, :], (P, 1))
    t["before"] = (i[:, None] < i[None, :]).astype(float)
    t["ones"] = np.ones((P, P))
    sc = np.zeros((P, 2))
    for s in range(2):
        sc[[s, 2 + s, 4], s] = 1.0
    t["selcol"] = sc
    t["iota8"] = np.tile(np.arange(NE)[None, :], (P, 1))
    t["left8"] = NE - t["iota8"]
    return np.concatenate([t[name] for name, _ in CONST_COLS], axis=1).astype(np.float32)


_INS = ['x', 'c', 'ctx', 'c_ctx', 'w_mod', 'b_mod', 'g_pre_mix', 'g_post_mix', 'g_pre_ffn', 'g_post_ffn', 'w_in', 'w_out',
        'w_fourier', 'win_sink', 'mla_g_q', 'mla_g_kv', 'mla_w_uq', 'mla_w_ukv', 'sgu_w', 'sgu_b', 'ffn_w_gate',
        'ffn_w_up', 'ffn_w_down', 'moe_w_router', 'moe_w_gate', 'moe_w_up', 'moe_w_down']


def kernel(**inputs):
    import concourse.bacc as bacc
    from concourse.bass_utils import run_bass_kernel_spmd

    nc = bacc.Bacc("TRN2", target_bir_lowering=False, num_devices=1)
    arrays = {f"in_{name}": np.ascontiguousarray(inputs[name]) for name in _INS}
    arrays["in_consts"] = shape_constants()
    args = [nc.dram_tensor(n, a.shape, mybir.dt.from_np(a.dtype), kind="ExternalInput").ap() for n, a in arrays.items()]
    out = nc.dram_tensor("out", (1, SEQ, D), F32, kind="ExternalOutput").ap()
    build(nc, *args, out)
    r = run_bass_kernel_spmd(nc, [arrays], core_ids=[0])
    return r.results[0]["out"]
```
